# Optimizing a Trainium2 kernel written in Bass

```python
import jax
import jax.numpy as jnp
from jax import lax
import numpy as np

D_MODEL = 1024
BATCH = 1
SEQ = 128
DEPTH = 2
DEC_BATCH = 1
DEC_SEQ = 512
PAST_LEN = 128

GRID_W = 64
HEAD_DIM = 64
N_HEADS_A = 8
N_KV_HEADS = 2
Q_PER_KV = N_HEADS_A // N_KV_HEADS
N_HEADS_R = 8
D_ATTN = N_HEADS_A * HEAD_DIM
D_KV = N_KV_HEADS * HEAD_DIM
D_RWKV = N_HEADS_R * HEAD_DIM
WINDOW = 128
BLOCK = 128
ROPE_BASE = 10000.0
DECAY_RANK = 64
ICLR_RANK = 64
GATE_RANK = 128
CONV_W = 3
DECAY_SCALE = 0.606531
GN_EPS = 64e-5
N_KEYS = 128
N_EXPERTS = N_KEYS * N_KEYS
PEER_HEADS = 8
PEER_TOPK = 16
D_QUERY = 256
HALF_Q = D_QUERY // 2
PEER_CHUNK = 128
N_MOD = 6
EPS = 1e-6
NEG_INF = -1e30
D_IN = D_ATTN + 2 * D_KV + 3 * D_RWKV + 2 * DECAY_RANK + 2 * ICLR_RANK + GATE_RANK

kernel_name = "hybrid_dit_swa_rwkv7_peer_step"

def _rms(x, g):
    xf = x.astype(jnp.float32)
    y = xf * lax.rsqrt(jnp.mean(xf * xf, axis=-1, keepdims=True) + EPS)
    return (y * g.astype(jnp.float32)).astype(x.dtype)

def _split_proj(z):
    sizes = (D_ATTN, D_KV, D_KV, 3 * D_RWKV, 2 * DECAY_RANK, 2 * ICLR_RANK, GATE_RANK)
    out = []
    o = 0
    for s in sizes:
        out.append(z[..., o:o + s])
        o += s
    return out

def _axial_rope(x):
    T = x.shape[1]
    rows = T // GRID_W
    row = jnp.repeat(jnp.arange(rows), GRID_W).astype(jnp.float32)
    col = jnp.tile(jnp.arange(GRID_W), rows).astype(jnp.float32)
    half = HEAD_DIM // 2
    quarter = half // 2
    freqs = ROPE_BASE ** (-jnp.arange(quarter, dtype=jnp.float32) / quarter)

    def rot(xa, pos):
        ang = pos[:, None] * freqs[None, :]
        cos = jnp.cos(ang)[None, :, None, :]
        sin = jnp.sin(ang)[None, :, None, :]
        x1 = xa[..., :quarter].astype(jnp.float32)
        x2 = xa[..., quarter:].astype(jnp.float32)
        return jnp.concatenate([x1 * cos - x2 * sin, x1 * sin + x2 * cos], axis=-1)

    out = jnp.concatenate([rot(x[..., :half], row), rot(x[..., half:], col)], axis=-1)
    return out.astype(x.dtype)

def _attend(q, k, v, valid, sink):
    s = jnp.einsum('bqgrd,bkgd->bgrqk', q, k).astype(jnp.float32) * (HEAD_DIM ** -0.5)
    if valid is not None:
        s = jnp.where(valid[None, None, None], s, NEG_INF)
    B, G, R, Q = s.shape[:4]
    sk = jnp.broadcast_to(sink.astype(jnp.float32)[None, :, :, None, None], (B, G, R, Q, 1))
    p = jax.nn.softmax(jnp.concatenate([s, sk], axis=-1), axis=-1)[..., :-1]
    return jnp.einsum('bgrqk,bkgd->bqgrd', p.astype(v.dtype), v)

def _context_attention(q, k, v, sink):
    B, S = q.shape[:2]
    nb = S // BLOCK
    qb = jnp.moveaxis(q.reshape(B, nb, BLOCK, N_KV_HEADS, Q_PER_KV, HEAD_DIM), 1, 0)
    out = lax.map(lambda qi: _attend(qi, k, v, None, sink), qb)
    return jnp.moveaxis(out, 0, 1).reshape(B, S, D_ATTN)

def _latent_attention(q, k, v, ck, cv, sink):
    B, T = q.shape[:2]
    P = ck.shape[1]
    nb = T // BLOCK
    pad = ((0, 0), (BLOCK, BLOCK), (0, 0), (0, 0))
    kp = jnp.pad(k, pad)
    vp = jnp.pad(v, pad)
    qb = jnp.moveaxis(q.reshape(B, nb, BLOCK, N_KV_HEADS, Q_PER_KV, HEAD_DIM), 1, 0)
    qoff = jnp.arange(BLOCK)
    koff = jnp.arange(3 * BLOCK) - BLOCK
    ctx_valid = jnp.ones((BLOCK, P), dtype=bool)

    def blk(args):
        qi, i = args
        start = i * BLOCK
        kl = lax.dynamic_slice_in_dim(kp, start, 3 * BLOCK, axis=1)
        vl = lax.dynamic_slice_in_dim(vp, start, 3 * BLOCK, axis=1)
        qpos = start + qoff
        kpos = start + koff
        band = (jnp.abs(qpos[:, None] - kpos[None, :]) <= WINDOW) & (kpos[None, :] >= 0) & (kpos[None, :] < T)
        valid = jnp.concatenate([band, ctx_valid], axis=1)
        return _attend(qi, jnp.concatenate([kl, ck], axis=1), jnp.concatenate([vl, cv], axis=1), valid, sink)

    out = lax.map(blk, (qb, jnp.arange(nb)))
    return jnp.moveaxis(out, 0, 1).reshape(B, T, D_ATTN)

def _centred_conv(x, w):
    T = x.shape[1]
    r = CONV_W // 2
    xp = jnp.pad(x, ((0, 0), (r, r), (0, 0)))
    out = xp[:, 0:T] * w[0]
    for j in range(1, CONV_W):
        out = out + xp[:, j:j + T] * w[j]
    return out

def _rwkv_step(S, inp):
    r, w, kk, a, k, v = inp
    sk = jnp.einsum('bdhvk,bdhk->bdhv', S, kk)
    S = S * w[..., None, :] - sk[..., :, None] * (kk * a)[..., None, :] + v[..., :, None] * k[..., None, :]
    return S, jnp.einsum('bdhvk,bdhk->bdhv', S, r)

def _rwkv(rkv, wd, ad, gd, s0, p):
    B, T, _ = rkv.shape
    rkv = _centred_conv(rkv, p['conv_rkv'])
    r, k, v = rkv[..., :D_RWKV], rkv[..., D_RWKV:2 * D_RWKV], rkv[..., 2 * D_RWKV:]
    wd = wd.reshape(B, T, 2, DECAY_RANK)
    ad = ad.reshape(B, T, 2, ICLR_RANK)
    w = jnp.exp(-DECAY_SCALE * jax.nn.sigmoid(p['w0'] + jnp.einsum('btdr,drc->btdc', jnp.tanh(wd), p['w2'])))
    a = jax.nn.sigmoid(p['a0'] + jnp.einsum('btdr,drc->btdc', ad, p['a2']))
    kk = (k * p['k_k']).reshape(B, T, N_HEADS_R, HEAD_DIM).astype(jnp.float32)
    kk = kk * lax.rsqrt(jnp.sum(kk * kk, axis=-1, keepdims=True) + EPS)
    kmod = k[:, :, None, :] * (1.0 + (a - 1.0) * p['k_a'])

    def per_dir(t):
        return t.reshape(B, T, 2, N_HEADS_R, HEAD_DIM)

    def shared(t):
        return jnp.broadcast_to(t.reshape(B, T, 1, N_HEADS_R, HEAD_DIM), (B, T, 2, N_HEADS_R, HEAD_DIM))

    def to_scan(t):
        t = jnp.stack([t[:, :, 0], jnp.flip(t[:, :, 1], axis=1)], axis=2)
        return jnp.moveaxis(t, 1, 0).astype(jnp.float32)

    xs = (to_scan(shared(r)), to_scan(per_dir(w)), to_scan(shared(kk)),
          to_scan(per_dir(a)), to_scan(per_dir(kmod)), to_scan(shared(v)))
    s_final, y = lax.scan(_rwkv_step, s0.astype(jnp.float32), xs)
    y = jnp.moveaxis(y, 0, 1)
    y = y[:, :, 0] + jnp.flip(y[:, :, 1], axis=1)
    mu = jnp.mean(y, axis=-1, keepdims=True)
    var = jnp.mean(jnp.square(y - mu), axis=-1, keepdims=True)
    yn = ((y - mu) * lax.rsqrt(var + GN_EPS)).reshape(B, T, D_RWKV)
    yn = (yn * p['ln_x_g'].astype(jnp.float32) + p['ln_x_b'].astype(jnp.float32)).astype(rkv.dtype)
    rh = r.reshape(B, T, N_HEADS_R, HEAD_DIM)
    kh = k.reshape(B, T, N_HEADS_R, HEAD_DIM)
    vh = v.reshape(B, T, N_HEADS_R, HEAD_DIM)
    bonus = (jnp.sum(rh * kh * p['r_k'], axis=-1, keepdims=True) * vh).reshape(B, T, D_RWKV)
    gate = jax.nn.sigmoid(gd) @ p['g2']
    return (yn + bonus) * gate, s_final.astype(rkv.dtype)

def _token_mixers(h, p, ck, cv, cstate):
    B, T, _ = h.shape
    q, k, v, rkv, wd, ad, gd = _split_proj(h @ p['w_in'])
    q = _rms(q.reshape(B, T, N_HEADS_A, HEAD_DIM), p['q_norm'])
    k = _rms(k.reshape(B, T, N_KV_HEADS, HEAD_DIM), p['k_norm'])
    v = v.reshape(B, T, N_KV_HEADS, HEAD_DIM)
    sink = p['sink'].reshape(N_KV_HEADS, Q_PER_KV)
    if ck is None:
        attn = _context_attention(q, k, v, sink)
        s0 = jnp.zeros((B, 2, N_HEADS_R, HEAD_DIM, HEAD_DIM), jnp.float32)
    else:
        attn = _latent_attention(_axial_rope(q), _axial_rope(k), v, ck, cv, sink)
        s0 = cstate
    rw, s_final = _rwkv(rkv, wd, ad, gd, s0, p)
    out = jnp.concatenate([attn, rw], axis=-1) @ p['w_out']
    if ck is None:
        return out, (k, v, s_final)
    return out, None

def _peer(h, p):
    B, T, D = h.shape
    n = B * T
    x = h.reshape(n, D)
    q = (x @ p['w_query']).reshape(n, PEER_HEADS, 2, HALF_Q)
    s = jnp.einsum('nhcq,ckq->nhck', q, p['sub_keys']).astype(jnp.float32)
    sv, si = lax.top_k(s, PEER_TOPK)
    cand = (sv[:, :, 0, :, None] + sv[:, :, 1, None, :]).reshape(n, PEER_HEADS, PEER_TOPK * PEER_TOPK)
    cidx = (si[:, :, 0, :, None] * N_KEYS + si[:, :, 1, None, :]).reshape(n, PEER_HEADS, PEER_TOPK * PEER_TOPK)
    top_s, top_j = lax.top_k(cand, PEER_TOPK)
    eidx = jnp.take_along_axis(cidx, top_j, axis=-1)
    g = jax.nn.softmax(top_s, axis=-1).astype(h.dtype)
    nc = n // PEER_CHUNK
    xc = x.reshape(nc, PEER_CHUNK, D)
    ec = eidx.reshape(nc, PEER_CHUNK, PEER_HEADS * PEER_TOPK)
    gc = g.reshape(nc, PEER_CHUNK, PEER_HEADS * PEER_TOPK)
    u_tab = p['expert_u']
    v_tab = p['expert_v']

    def chunk(args):
        xi, ei, gi = args
        act = jax.nn.gelu(jnp.einsum('ced,cd->ce', u_tab[ei], xi))
        return jnp.einsum('ce,ced->cd', gi * act, v_tab[ei])

    y = lax.map(chunk, (xc, ec, gc))
    return y.reshape(B, T, D)

def _layer(x, cond, p, ck, cv, cstate):
    mod = jax.nn.silu(cond) @ p['w_mod'] + p['b_mod']
    sh1, sc1, g1, sh2, sc2, g2 = jnp.split(mod, N_MOD, axis=-1)
    h = _rms(x, p['norm1']) * (1.0 + sc1) + sh1
    out, ctx = _token_mixers(h, p, ck, cv, cstate)
    x = x + g1 * out
    h = _rms(x, p['norm2']) * (1.0 + sc2) + sh2
    x = x + g2 * _peer(h, p)
    return x, ctx

def setup_inputs(seed: int = 0) -> dict:
    key = jax.random.key(seed)
    ks = jax.random.split(key, 40)

    def nrm(k, shape, scale):
        return scale * jax.random.normal(k, shape, jnp.float32)

    centre = jnp.zeros((CONV_W,), jnp.float32).at[CONV_W // 2].set(1.0)
    return {
        'x_prompt': nrm(ks[0], (BATCH, SEQ, D_MODEL), 1.0),
        'x_sample': nrm(ks[1], (DEC_BATCH, DEC_SEQ, D_MODEL), 1.0),
        'cache_k': nrm(ks[2], (DEC_BATCH, DEPTH, PAST_LEN, N_KV_HEADS, HEAD_DIM), 1.0),
        'cache_v': nrm(ks[3], (DEC_BATCH, DEPTH, PAST_LEN, N_KV_HEADS, HEAD_DIM), 1.0),
        'state_rwkv': nrm(ks[4], (DEC_BATCH, DEPTH, 2, N_HEADS_R, HEAD_DIM, HEAD_DIM), 0.3),
        'c': nrm(ks[5], (DEC_BATCH, D_MODEL), 1.0),
        'c_ctx': nrm(ks[6], (D_MODEL,), 1.0),
        'w_mod': nrm(ks[7], (DEPTH, D_MODEL, N_MOD * D_MODEL), 0.5 * D_MODEL ** -0.5),
        'b_mod': nrm(ks[8], (DEPTH, N_MOD * D_MODEL), 0.02),
        'norm1': 1.0 + nrm(ks[9], (DEPTH, D_MODEL), 0.05),
        'norm2': 1.0 + nrm(ks[10], (DEPTH, D_MODEL), 0.05),
        'w_in': nrm(ks[11], (DEPTH, D_MODEL, D_IN), D_MODEL ** -0.5),
        'q_norm': 1.0 + nrm(ks[12], (DEPTH, HEAD_DIM), 0.05),
        'k_norm': 1.0 + nrm(ks[13], (DEPTH, HEAD_DIM), 0.05),
        'sink': nrm(ks[14], (DEPTH, N_HEADS_A), 0.5),
        'conv_rkv': centre[None, :, None] + nrm(ks[15], (DEPTH, CONV_W, 3 * D_RWKV), 0.2),
        'w0': nrm(ks[16], (DEPTH, 2, D_RWKV), 1.0),
        'w2': nrm(ks[17], (DEPTH, 2, DECAY_RANK, D_RWKV), DECAY_RANK ** -0.5),
        'a0': nrm(ks[18], (DEPTH, 2, D_RWKV), 0.5),
        'a2': nrm(ks[19], (DEPTH, 2, ICLR_RANK, D_RWKV), ICLR_RANK ** -0.5),
        'g2': nrm(ks[20], (DEPTH, GATE_RANK, D_RWKV), GATE_RANK ** -0.5),
        'k_k': 0.85 + nrm(ks[21], (DEPTH, D_RWKV), 0.05),
        'k_a': 1.0 + nrm(ks[22], (DEPTH, D_RWKV), 0.05),
        'r_k': nrm(ks[23], (DEPTH, N_HEADS_R, HEAD_DIM), 0.1),
        'ln_x_g': 1.0 + nrm(ks[24], (DEPTH, D_RWKV), 0.05),
        'ln_x_b': nrm(ks[25], (DEPTH, D_RWKV), 0.02),
        'w_out': nrm(ks[26], (DEPTH, D_MODEL, D_MODEL), D_MODEL ** -0.5),
        'w_query': nrm(ks[27], (DEPTH, D_MODEL, PEER_HEADS * D_QUERY), D_MODEL ** -0.5),
        'sub_keys': nrm(ks[28], (DEPTH, 2, N_KEYS, HALF_Q), HALF_Q ** -0.5),
        'expert_u': nrm(ks[29], (DEPTH, N_EXPERTS, D_MODEL), D_MODEL ** -0.5),
        'expert_v': nrm(ks[30], (DEPTH, N_EXPERTS, D_MODEL), PEER_HEADS ** -0.5),
    }

def reference(x_prompt, x_sample, cache_k, cache_v, state_rwkv, c, c_ctx, w_mod, b_mod, norm1, norm2,
              w_in, q_norm, k_norm, sink, conv_rkv, w0, w2, a0, a2, g2, k_k, k_a, r_k, ln_x_g, ln_x_b,
              w_out, w_query, sub_keys, expert_u, expert_v):
    cond_ctx = c_ctx[None, None, :]
    cond_lat = c[:, None, :]
    yp = x_prompt
    ys = x_sample
    ks_out, vs_out, ss_out = [], [], []
    for i in range(DEPTH):
        p = {
            'w_mod': w_mod[i], 'b_mod': b_mod[i], 'norm1': norm1[i], 'norm2': norm2[i],
            'w_in': w_in[i], 'q_norm': q_norm[i], 'k_norm': k_norm[i], 'sink': sink[i],
            'conv_rkv': conv_rkv[i], 'w0': w0[i], 'w2': w2[i], 'a0': a0[i], 'a2': a2[i],
            'g2': g2[i], 'k_k': k_k[i], 'k_a': k_a[i], 'r_k': r_k[i],
            'ln_x_g': ln_x_g[i], 'ln_x_b': ln_x_b[i], 'w_out': w_out[i],
            'w_query': w_query[i], 'sub_keys': sub_keys[i],
            'expert_u': expert_u[i], 'expert_v': expert_v[i],
        }
        yp, ctx = _layer(yp, cond_ctx, p, None, None, None)
        ks_out.append(ctx[0])
        vs_out.append(ctx[1])
        ss_out.append(ctx[2])
        ys, _ = _layer(ys, cond_lat, p, cache_k[:, i], cache_v[:, i], state_rwkv[:, i])
    new_cache_k = jnp.stack(ks_out, axis=1)
    new_cache_v = jnp.stack(vs_out, axis=1)
    new_state_rwkv = jnp.stack(ss_out, axis=1)
    return (yp, ys, new_cache_k, new_cache_v, new_state_rwkv)


_drawn_inputs = setup_inputs


def setup_inputs(seed=0):
    import zlib

    import numpy as np

    out = dict(_drawn_inputs(seed))
    spreads = {}
    factors = {'cache_k': 3.29,
     'cache_v': 2.732,
     'state_rwkv': 8.0,
     'norm2': 2.788,
     'q_norm': 8.0,
     'sink': 64.0,
     'k_k': 4.193,
     'ln_x_g': 5.019,
     'ln_x_b': 8.0}
    for name, (base, spread) in spreads.items():
        noise = np.random.default_rng([zlib.crc32(name.encode()), seed]).standard_normal(out[name].shape)
        drawn = base * np.exp(spread * noise) if base else spread * noise
        out[name] = jnp.asarray(drawn.astype(out[name].dtype))
    for name, factor in factors.items():
        out[name] = (out[name] * factor).astype(out[name].dtype)
    return out
```

```python
from contextlib import ExitStack, contextmanager

import numpy as np

import concourse.bass as bass
from concourse import mybir

F32 = mybir.dt.float32
F32R = mybir.dt.float32r
BF16 = mybir.dt.bfloat16
U32 = mybir.dt.uint32
ALU = mybir.AluOpType
ACT = mybir.ActivationFunctionType
AX = mybir.AxisListType

P = 128
D = 1024
KB = D // P
CTX, LAT = 128, 512
T = CTX + LAT
TILES = T // P
HALF = T // 2
LAYERS = 2
HD = 64
HEADS = 8
D_R = 512
RB = D_R // P
IN_BLOCKS = 21
Q_BLOCKS = 16
OUT_BLOCKS = 8
W_BLOCKS = IN_BLOCKS + OUT_BLOCKS + Q_BLOCKS
Z_K, Z_V, Z_RKV, Z_WD, Z_AD, Z_GD = 4, 5, 6, 18, 19, 20
N_KEYS = 128
TOPK = 16
EPS = 1e-6
GN_EPS = 64e-5
DECAY = 0.606531
CHUNK = 64
LEVELS = 6
N_MASKS = 3 + LEVELS
MIN_F32 = -3.0e38
FIRST_SEM = 110
SEGMENTS = ((0, 0, CTX), (1, CTX, T))

_PV = [("norm1", KB), ("norm2", KB), ("q_norm", 1), ("k_norm", 1), ("conv", 36), ("a0", 8),
       ("k_k", 4), ("k_a", 4), ("r_k", 4), ("ln_g", 4), ("ln_b", 4), ("b_mod", 48), ("sink", 8)]
PV = {}
_at = 0
for _n, _w in _PV:
    PV[_n] = (_at, _at + _w)
    _at += _w
NPV = _at


@contextmanager
def stage(nc, *names):
    sems = [nc.alloc_semaphore(n, num=FIRST_SEM + i) for i, n in enumerate(names)]
    with nc.Block(name="stage_" + names[0], no_gpsimd_drain=True) as block:
        yield (block, *sems)
    nc.all_engine_barrier(sems_to_clear=range(FIRST_SEM, FIRST_SEM + len(sems)))
    for sem in sems:
        nc.release_semaphore(sem)


class Names:
    pass


class Chain:

    def __init__(self, eng, sem, base=0):
        self.eng, self.sem, self.base, self.n = eng, sem, base, 0

    def __call__(self, ins):
        self.n += 1
        ins.then_inc(self.sem, 1)
        self.eng.wait_ge(self.sem, self.base + self.n)

    def mark(self, ins):
        self.n += 1
        ins.then_inc(self.sem, 1)
        return self.base + self.n


def bcast(ap, axis, n):
    ap = ap.unsqueeze(axis)
    shape = list(ap.shape)
    shape[axis] = n
    return ap.broadcast_to(shape)


def load_constants(nc, s):
    with ExitStack() as mem:
        cond = mem.enter_context(nc.sbuf_tensor("cond", [P, KB, 2], F32))
        tanh_c = mem.enter_context(nc.sbuf_tensor("tanh_c", [P, KB, 2], F32))
        with stage(nc, "c_loaded", "c_tanh", "c_chain") as (block, loaded, tanhed, chain):
            @block.sync
            def _(sp):
                for dst, src in ((s.x, s.d["x_in"]), (cond, s.d["cond"]), (s.ones, s.d["ones"]), (s.blk, s.d["blk"]),
                                 (s.ident, s.d["ident"])):
                    sp.dma_start(dst[:], src).then_inc(loaded, 16)
                sp.wait_ge(loaded, 80)

            @block.scalar
            def _(act):
                act.wait_ge(loaded, 80)
                nc.scalar.activation(tanh_c[:], cond[:], ACT.Tanh, scale=0.5).then_inc(tanhed, 1)

            @block.vector
            def _(dve):
                link = Chain(dve, chain)
                dve.wait_ge(loaded, 80)
                dve.wait_ge(tanhed, 1)
                link(nc.vector.tensor_scalar(tanh_c[:], tanh_c[:], 0.5, 0.5, ALU.mult, ALU.add))
                link(nc.vector.tensor_tensor(cond[:], cond[:], tanh_c[:], ALU.mult))
                link(nc.vector.tensor_copy(s.silu_parts[:, :, 0:2], cond[:]))
                nc.vector.tensor_tensor(s.silu_parts[:, :, 2:4], cond[:], s.silu_parts[:, :, 0:2].bitcast(F32),
                                        ALU.subtract)


def modulation(nc, s, layer):
    CH = 4
    N = 48 // CH
    W = CH * P
    U = 3
    with ExitStack() as mem:
        w = mem.enter_context(nc.sbuf_tensor("mod_w", [P, U, KB, W], F32))
        w_hi = mem.enter_context(nc.sbuf_tensor("mod_w_hi", [P, U, KB, W], F32R))
        w_lo = mem.enter_context(nc.sbuf_tensor("mod_w_lo", [P, U, KB, W], F32R))
        rows = mem.enter_context(nc.sbuf_tensor("mod_rows", [4, U, W], F32))
        ps = mem.enter_context(nc.psum_tensor("mod_ps", [4, U, W], F32))
        ps_t = mem.enter_context(nc.psum_tensor("mod_ps_t", [P, 48 * 4], F32))
        with stage(nc, "mod_pv", *["mod_w%d" % u for u in range(U)], "mod_hi", "mod_split", "mod_done", "mod_rows", "mod_turned",
                   "mod_chain") as (block, pv_loaded, *sems):
            w_loaded, (hi_ready, split, done, rows_ready, turned, chain) = sems[:U], sems[U:]

            @block.sync
            def _(sp):
                sp.dma_start(s.pv[:], s.d["pv"][bass.ds(layer, 1)].rearrange("a p n -> p (a n)")).then_inc(pv_loaded, 16)
                with sp.Fori(0, N // U) as i:
                    for u in range(U):
                        sp.wait_ge(split, i * U + u + 1)
                        sp.dma_start(w[:, u], s.d["w_mod"][bass.ds(layer * N + i * U + u, 1)]
                                     .rearrange("a p k n -> p (a k) n")).then_inc(w_loaded[u], 16)

            @block.scalar
            def _(act):
                act.sem_inc(rows_ready, U)

                def high(n, turn, u):
                    act.wait_ge(w_loaded[u], turn * 16 + 16)
                    act.wait_ge(done, n + 1)
                    nc.scalar.activation(w_hi[:, u], w[:, u], ACT.Copy).then_inc(hi_ready, 1)

                def take(n, u):
                    act.wait_ge(done, n + U + 1)
                    act.wait_ge(turned, n + 1)
                    nc.scalar.activation(rows[:, u], ps[:, u], ACT.Copy).then_inc(rows_ready, 1)

                high(0, 0, 0)
                with act.Fori(0, N // U - 1) as i:
                    for u in range(U):
                        high(i * U + u + 1, i + (u + 1) // U, (u + 1) % U)
                        take(i * U + u, u)
                for u in range(U):
                    if u + 1 < U:
                        high(N - U + u + 1, N // U - 1, u + 1)
                    take(N - U + u, u)

            @block.tensor
            def _(pe):
                pe.sem_inc(done, U)
                pe.sem_inc(turned, U)

                def product(n, u):
                    pe.wait_ge(split, n + U + 1)
                    pe.wait_ge(rows_ready, n + 1)
                    for kb in range(KB):
                        for part in (w_hi, w_lo):
                            last = nc.tensor.matmul(ps[:, u], s.silu_parts[:, kb, :], part[:, u, kb, :],
                                                    start=(kb == 0 and part is w_hi),
                                                    stop=(kb == KB - 1 and part is w_lo))
                    last.then_inc(done, 1)

                def turn(n, u):
                    pe.wait_ge(rows_ready, n + U + 1)
                    for c in range(CH):
                        last = nc.tensor.matmul(ps_t[:, bass.ds(n * (4 * CH) + 4 * c, 4)],
                                                rows[:, u, c * P:(c + 1) * P], s.ident[0:4, 0:4], start=True, stop=True)
                    last.then_inc(turned, 1)

                product(0, 0)
                with pe.Fori(0, N // U - 1) as i:
                    for u in range(U):
                        product(i * U + u + 1, (u + 1) % U)
                        turn(i * U + u, u)
                for u in range(U):
                    if u + 1 < U:
                        product(N - U + u + 1, u + 1)
                    turn(N - U + u, u)

            @block.vector
            def _(dve):
                link = Chain(dve, chain)
                dve.sem_inc(split, U)
                with dve.Fori(0, N // U) as i:
                    for u in range(U):
                        dve.wait_ge(hi_ready, i * U + u + 1)
                        nc.vector.tensor_tensor(w_lo[:, u], w[:, u], w_hi[:, u].bitcast(F32),
                                                ALU.subtract).then_inc(split, 1)
                dve.wait_ge(pv_loaded, 16)
                dve.wait_ge(turned, N + U)
                parts = ps_t[:].rearrange("p (b h c) -> p b h c", h=2, c=2)
                link(nc.vector.tensor_tensor(s.mod[:], parts[:, :, 1, :], bcast(s.pvs("b_mod"), 2, 2), ALU.add))
                link(nc.vector.tensor_tensor(s.mod[:], s.mod[:], parts[:, :, 0, :], ALU.add))
                for gain, norm, scale in ((s.gain1, "norm1", KB), (s.gain2, "norm2", 4 * KB)):
                    link(nc.vector.tensor_scalar(gain[:], s.mod[:, scale:scale + KB, :], 1.0, None, ALU.add))
                    link(nc.vector.tensor_tensor(gain[:], gain[:], bcast(s.pvs(norm), 2, 2), ALU.mult))


def rms_modulate(nc, s, name, gain, shift, hi, lo):
    with ExitStack() as mem:
        sq = mem.enter_context(nc.sbuf_tensor(name + "_sq", [P, 2, T], F32))
        r = mem.enter_context(nc.sbuf_tensor(name + "_r", [P, T], F32))
        h = mem.enter_context(nc.sbuf_tensor(name + "_h", [P, 2, T], F32))
        ps = mem.enter_context(nc.psum_tensor(name + "_ps", [P, 2, 512], F32))
        with stage(nc, name + "_sq_ready", name + "_summed", name + "_ms", name + "_root", name + "_h_ready",
                   name + "_hi_ready", name + "_chain") as \
                (block, sq_ready, summed, ms_ready, root, h_ready, hi_ready, chain):
            @block.scalar
            def _(act):
                for kb in range(KB):
                    if kb >= 2:
                        act.wait_ge(summed, kb - 1)
                    nc.scalar.activation(sq[:, kb % 2], s.x[:, kb], ACT.Square).then_inc(sq_ready, 1)
                act.wait_ge(ms_ready, 1)
                nc.scalar.activation(r[:], r[:], ACT.Sqrt).then_inc(root, 1)
                for kb in range(KB):
                    act.wait_ge(h_ready, kb + 1)
                    nc.scalar.activation(hi[:, kb], h[:, kb % 2], ACT.Copy).then_inc(hi_ready, 1)

            @block.tensor
            def _(pe):
                for kb in range(KB):
                    pe.wait_ge(sq_ready, kb + 1)
                    for q in range(2):
                        last = nc.tensor.matmul(ps[:, q, 0:HALF], s.ones[:], sq[:, kb % 2, q * HALF:(q + 1) * HALF],
                                                start=(kb == 0), stop=(kb == KB - 1))
                    last.then_inc(summed, 1)

            @block.vector
            def _(dve):
                link = Chain(dve, chain)
                dve.wait_ge(summed, KB)
                nc.vector.tensor_scalar(r[:].rearrange("p (q n) -> p q n", q=2), ps[:, :, 0:HALF],
                                        1.0 / D, EPS, ALU.mult, ALU.add).then_inc(ms_ready, 1)
                dve.wait_ge(root, 1)
                link(nc.vector.reciprocal(r[:], r[:]))
                for kb in range(KB):
                    if kb >= 2:
                        dve.wait_ge(hi_ready, kb - 1)
                    link(nc.vector.tensor_tensor(h[:, kb % 2], s.x[:, kb], r[:], ALU.mult))
                    for c, a, b in SEGMENTS:
                        last = nc.vector.tensor_scalar(h[:, kb % 2, a:b], h[:, kb % 2, a:b], gain[:, kb, c:c + 1],
                                                       s.mod[:, shift + kb, c:c + 1], ALU.mult, ALU.add)
                        if c == 0:
                            link(last)
                    last.then_inc(h_ready, 1)
                    dve.wait_ge(hi_ready, kb + 1)
                    link(nc.vector.tensor_tensor(lo[:, kb], h[:, kb % 2], hi[:, kb].bitcast(F32), ALU.subtract))


def matmul_split(nc, out, w_hi, w_lo, hi, lo, first, last):
    terms = ((w_hi, hi), (w_hi, lo), (w_lo, hi))
    for n, (a, b) in enumerate(terms):
        for q in range(2):
            ins = nc.tensor.matmul(out[:, q, 0:HALF], a, b[:, q * HALF:(q + 1) * HALF],
                                   start=(first and n == 0), stop=(last and n == 2))
    return ins


def project(nc, s, name, layer, first_block, n_blocks, unroll, hi, lo, evacuate, scores=None):
    U = unroll
    with ExitStack() as mem:
        raw = mem.enter_context(nc.sbuf_tensor(name + "_raw", [P, U, KB, P], F32))
        w_hi = mem.enter_context(nc.sbuf_tensor(name + "_whi", [P, U, KB, P], F32R))
        w_lo = mem.enter_context(nc.sbuf_tensor(name + "_wlo", [P, U, KB, P], F32R))
        ps = mem.enter_context(nc.psum_tensor(name + "_ps", [P, U, 2, 512], F32))
        extra = ("sc_done", "sc_taken", "sc_chain") if scores else ()
        with stage(nc, *[name + "_loaded%d" % u for u in range(U)], name + "_hi_ready", name + "_split",
                   name + "_done", name + "_taken", *[name + "_" + e for e in extra]) as (block, *sems):
            loaded, (hi_ready, split, done, taken), more = sems[:U], sems[U:U + 4], sems[U + 4:]

            @block.sync
            def _(sp):
                with sp.Fori(0, n_blocks // U) as i:
                    for u in range(U):
                        sp.wait_ge(split, i * U + u + 1)
                        sp.dma_start(raw[:, u], s.d["w_blocks"][bass.ds(layer * W_BLOCKS + first_block + i * U + u, 1)]
                                     .rearrange("a p k n -> p (a k) n")).then_inc(loaded[u], 16)

            @block.scalar
            def _(act):
                act.sem_inc(taken, U)
                with act.Fori(0, n_blocks // U) as i:
                    for u in range(U):
                        act.wait_ge(loaded[u], (i + 1) * 16)
                        act.wait_ge(done, i * U + u + 1)
                        nc.scalar.activation(w_hi[:, u], raw[:, u], ACT.Copy).then_inc(hi_ready, 1)
                    for u in range(U):
                        act.wait_ge(done, i * U + U + u + 1)
                        evacuate(act, i, u, ps[:, u], *more).then_inc(taken, 1)

            @block.vector
            def _(dve):
                dve.sem_inc(split, U)
                if scores:
                    dve.sem_inc(more[1], U)

                def low_parts(i):
                    for u in range(U):
                        dve.wait_ge(hi_ready, i * U + u + 1)
                        nc.vector.tensor_tensor(w_lo[:, u], raw[:, u], w_hi[:, u].bitcast(F32),
                                                ALU.subtract).then_inc(split, 1)

                if scores:
                    low_parts(0)
                    with dve.Fori(0, n_blocks // U - 1) as i:
                        low_parts(i + 1)
                        scores[1](dve, i, *more)
                    scores[1](dve, n_blocks // U - 1, *more)
                else:
                    with dve.Fori(0, n_blocks // U) as i:
                        low_parts(i)

            @block.tensor
            def _(pe):
                pe.sem_inc(done, U)
                if scores:
                    pe.sem_inc(more[0], U)
                with pe.Fori(0, n_blocks // U) as i:
                    for u in range(U):
                        pe.wait_ge(split, i * U + U + u + 1)
                        pe.wait_ge(taken, i * U + u + 1)
                        for kb in range(KB):
                            ins = matmul_split(nc, ps[:, u], w_hi[:, u, kb], w_lo[:, u, kb], hi[:, kb], lo[:, kb],
                                               kb == 0, kb == KB - 1)
                        ins.then_inc(done, 1)
                    if scores:
                        scores[0](pe, i, taken, *more)


def input_projection(nc, s, layer, hi, lo):
    def evacuate(act, i, u, ps):
        return nc.scalar.activation(s.z[:, bass.ds(i * 3 + u, 1), :].rearrange("p a (q n) -> p (a q) n", q=2),
                                    ps[:, :, 0:HALF], ACT.Copy)
    project(nc, s, "in", layer, 0, IN_BLOCKS, 3, hi, lo, evacuate)


def head_norm(nc, s, name, blocks, n_blocks, piece, mean_scale, eps, finish):
    cols = n_blocks * T
    pieces = cols // piece
    with ExitStack() as mem:
        sq = mem.enter_context(nc.sbuf_tensor(name + "_sq", [P, cols], F32))
        ps = mem.enter_context(nc.psum_tensor(name + "_ps", [P, pieces, 512], F32))
        with stage(nc, name + "_sq_ready", name + "_summed", name + "_ms", name + "_root", name + "_chain") as \
                (block, sq_ready, summed, ms_ready, root, chain):
            @block.scalar
            def _(act):
                nc.scalar.activation(sq[:], blocks, ACT.Square).then_inc(sq_ready, 1)
                act.wait_ge(ms_ready, 1)
                nc.scalar.activation(sq[:], sq[:], ACT.Sqrt).then_inc(root, 1)

            @block.tensor
            def _(pe):
                pe.wait_ge(sq_ready, 1)
                for n in range(pieces):
                    last = nc.tensor.matmul(ps[:, n, 0:piece], s.blk[:], sq[:, n * piece:(n + 1) * piece],
                                            start=True, stop=True)
                last.then_inc(summed, 1)

            @block.vector
            def _(dve):
                link = Chain(dve, chain)
                dve.wait_ge(summed, 1)
                nc.vector.tensor_scalar(sq[:].rearrange("p (n c) -> p n c", n=pieces), ps[:, :, 0:piece],
                                        mean_scale, eps, ALU.mult, ALU.add).then_inc(ms_ready, 1)
                dve.wait_ge(root, 1)
                link(nc.vector.reciprocal(sq[:], sq[:]))
                link(nc.vector.tensor_tensor(blocks, blocks, sq[:], ALU.mult))
                finish(dve, link)


def attention(nc, s, layer):
    qk = s.z[:, 0:5, :].rearrange("p b t -> p (b t)")

    def gains(dve, link):
        link(nc.vector.tensor_scalar(s.z[:, 0:4, :], s.z[:, 0:4, :], s.pvs("q_norm"), HD ** -0.5, ALU.mult, ALU.mult))
        link(nc.vector.tensor_scalar(s.z[:, Z_K, :], s.z[:, Z_K, :], s.pvs("k_norm"), None, ALU.mult))

    head_norm(nc, s, "qk", qk, 5, 400, 1.0 / HD, EPS, gains)

    with ExitStack() as mem:
        def sb(name, shape):
            return mem.enter_context(nc.sbuf_tensor("at_" + name, shape, F32))

        rope = sb("rope", [P, 2, LAT])
        swap = sb("swap", [P, P])
        rot = sb("rot", [P, 5, LAT])
        k_tiles = sb("k_tiles", [P, 7, P])
        v_tiles = sb("v_tiles", [P, 7, P])
        ck = sb("ck", [P, P])
        cv = sb("cv", [P, P])
        with mem.enter_context(ExitStack()) as inner:
            ps = inner.enter_context(nc.psum_tensor("rope_ps", [P, 5, LAT], F32))
            ps_v = inner.enter_context(nc.psum_tensor("rope_psv", [P, 2, 4 * P], F32))
            with stage(nc, "rope_loaded", "rope_kv_out", "rope_rotated", "rope_v_ready", "rope_cos",
                       "rope_chain", "rope_v_taken") as \
                    (block, loaded, kv_out, rotated, v_ready, cos_done, chain, v_taken):
                @block.sync
                def _(sp):
                    for dst, src in ((rope, s.d["rope"]), (swap, s.d["swap"]),
                                     (ck, s.d["cache_k"][bass.ds(layer, 1)].rearrange("a p n -> p (a n)")),
                                     (cv, s.d["cache_v"][bass.ds(layer, 1)].rearrange("a p n -> p (a n)"))):
                        sp.dma_start(dst[:], src).then_inc(loaded, 16)
                    sp.dma_start(s.d["kv_out"][bass.ds(layer, 1)].rearrange("a p b n -> p (a b) n"),
                                 s.z[:, Z_K:Z_V + 1, 0:CTX]).then_inc(kv_out, 16)
                    sp.wait_ge(kv_out, 16)

                @block.tensor
                def _(pe):
                    pe.wait_ge(loaded, 64)
                    for b in range(5):
                        last = nc.tensor.matmul(ps[:, b, :], swap[:], s.z[:, b, CTX:T], start=True, stop=True)
                    last.then_inc(rotated, 1)
                    for m in range(TILES):
                        last = nc.tensor.transpose(ps_v[:, m // 4, (m % 4) * P:(m % 4 + 1) * P],
                                                   s.z[:, Z_V, m * P:(m + 1) * P], s.ident[:])
                    last.then_inc(v_ready, 1)

                @block.gpsimd
                def _(pool):
                    pool.wait_ge(loaded, 64)
                    pool.wait_ge(rotated, 1)
                    nc.gpsimd.tensor_tensor(s.z[:, 3:5, CTX:T], s.z[:, 3:5, CTX:T], bcast(rope[:, 0], 1, 2),
                                            ALU.mult).then_inc(cos_done, 1)

                @block.scalar
                def _(act):
                    act.wait_ge(v_ready, 1)
                    nc.scalar.activation(v_tiles[:, 0, :], ps_v[:, 0, 0:P], ACT.Copy).then_inc(v_taken, 1)
                    nc.scalar.activation(v_tiles[:, 2:5, :].rearrange("p a n -> p (a n)"), ps_v[:, 0, P:4 * P],
                                         ACT.Copy).then_inc(v_taken, 1)
                    nc.scalar.activation(v_tiles[:, 5, :], ps_v[:, 1, 0:P], ACT.Copy).then_inc(v_taken, 1)

                @block.vector
                def _(dve):
                    link = Chain(dve, chain)
                    for m in (1, 6):
                        dve_m = nc.vector.memset(k_tiles[:, m, :], 0.0)
                        link(dve_m)
                        link(nc.vector.memset(v_tiles[:, m, :], 0.0))
                    dve.wait_ge(kv_out, 16)
                    dve.wait_ge(rotated, 1)
                    link(nc.vector.tensor_tensor(rot[:], ps[:], bcast(rope[:, 1], 1, 5), ALU.mult))
                    link(nc.vector.tensor_tensor(s.z[:, 0:3, CTX:T], s.z[:, 0:3, CTX:T], bcast(rope[:, 0], 1, 3),
                                                 ALU.mult))
                    dve.wait_ge(cos_done, 1)
                    link(nc.vector.tensor_tensor(s.z[:, 0:5, CTX:T], s.z[:, 0:5, CTX:T], rot[:], ALU.add))
                    link(nc.vector.tensor_copy(k_tiles[:, 0, :], s.z[:, Z_K, 0:CTX]))
                    link(nc.vector.tensor_copy(k_tiles[:, 2:6, :].rearrange("p a n -> p (a n)"), s.z[:, Z_K, CTX:T]))

        mask = sb("mask", [P, 4 * P])
        qs = sb("qs", [P, 4, P])
        ks = sb("ks", [P, 3 * P])
        vs = sb("vs", [P, 3, P])
        sm = sb("sm", [P, HEADS, 4 * P])
        pt = sb("pt", [P, 2, 4 * P])
        top = sb("top", [P, HEADS])
        sink_e = sb("sink_e", [P, HEADS])
        den = sb("den", [P, HEADS])
        ps_s = mem.enter_context(nc.psum_tensor("at_ps_s", [P, 2, 4 * P], F32))
        ps_t = mem.enter_context(nc.psum_tensor("at_ps_t", [P, 2, 4 * P], F32))
        ps_o = mem.enter_context(nc.psum_tensor("at_ps_o", [P, 4, P], F32))
        with nc.Fori(0, TILES) as m:
            with stage(nc, "at_mask", "at_staged", "at_scores", "at_masked", "at_top", "at_exp",
                       "at_probs", "at_pt_ready", "at_pt_taken", "at_out", "at_chain") as \
                    (block, mask_in, staged, scores, masked, top_ready, exped, probs, pt_ready, pt_taken, out_ready,
                     chain):
                @block.sync
                def _(sp):
                    sp.dma_start(mask[:], s.d["masks"][bass.ds(m, 1)].rearrange("a p n -> p (a n)")).then_inc(mask_in, 16)

                def values(pe, h):
                    g, b = h // 4, h % 4
                    pe.wait_ge(pt_taken, h + 1)
                    for k in range(4):
                        v_k = (vs[:, k, :] if k < 3 else cv[:])[:, g * HD:(g + 1) * HD]
                        last = nc.tensor.matmul(ps_o[g * HD:(g + 1) * HD, b, :], v_k,
                                                pt[:, h % 2, k * P:(k + 1) * P], start=(k == 0), stop=(k == 3))
                    last.then_inc(out_ready, 1)

                @block.tensor
                def _(pe):
                    pe.wait_ge(staged, 1)
                    for h in range(HEADS):
                        g, b = h // 4, h % 4
                        if h >= 2:
                            pe.wait_ge(masked, h - 1)
                        q_h = qs[g * HD:(g + 1) * HD, b, :]
                        nc.tensor.matmul(ps_s[:, h % 2, 0:3 * P], q_h, ks[g * HD:(g + 1) * HD, :], start=True,
                                         stop=True)
                        nc.tensor.matmul(ps_s[:, h % 2, 3 * P:4 * P], q_h, ck[g * HD:(g + 1) * HD, :], start=True,
                                         stop=True).then_inc(scores, 1)
                    for h in range(HEADS):
                        pe.wait_ge(probs, h + 1)
                        if h >= 2:
                            pe.wait_ge(pt_taken, h - 1)
                        for k in range(4):
                            last = nc.tensor.transpose(ps_t[:, h % 2, k * P:(k + 1) * P],
                                                       sm[:, h, k * P:(k + 1) * P], s.ident[:])
                        last.then_inc(pt_ready, 1)
                        if h >= 1:
                            values(pe, h - 1)
                    values(pe, HEADS - 1)

                @block.vector
                def _(dve):
                    link = Chain(dve, chain)
                    nc.vector.tensor_copy(qs[:], s.z[:, 0:4, bass.ds(m * P, P)])
                    nc.vector.tensor_copy(ks[:], k_tiles[:].rearrange("p a n -> p (a n)")[:, bass.ds(m * P, 3 * P)])
                    nc.vector.tensor_copy(vs[:], v_tiles[:, bass.ds(m, 3), :]).then_inc(staged, 1)
                    dve.wait_ge(mask_in, 16)
                    for h in range(HEADS):
                        dve.wait_ge(scores, h + 1)
                        nc.vector.tensor_tensor_reduce(sm[:, h, :], ps_s[:, h % 2, :], mask[:], 1.0,
                                                       s.pvs("sink")[:, h:h + 1], ALU.add, ALU.max,
                                                       top[:, h:h + 1]).then_inc(masked, 1)
                    dve.wait_ge(masked, HEADS)
                    link(nc.vector.tensor_scalar(top[:], top[:], -1.0, None, ALU.mult))
                    nc.vector.tensor_tensor(sink_e[:], s.pvs("sink"), top[:], ALU.add).then_inc(top_ready, 1)
                    dve.wait_ge(exped, HEADS + 1)
                    link(nc.vector.tensor_tensor(den[:], den[:], sink_e[:], ALU.add))
                    link(nc.vector.reciprocal(den[:], den[:]))
                    for h in range(HEADS):
                        nc.vector.tensor_scalar(sm[:, h, :], sm[:, h, :], den[:, h:h + 1], None,
                                                ALU.mult).then_inc(probs, 1)
                    dve.wait_ge(out_ready, HEADS)
                    nc.vector.tensor_copy(s.mix[:, 0:4, bass.ds(m * P, P)], ps_o[:])

                @block.scalar
                def _(act):
                    act.wait_ge(top_ready, 1)
                    nc.scalar.activation(sink_e[:], sink_e[:], ACT.Exp).then_inc(exped, 1)
                    for h in range(HEADS):
                        nc.scalar.activation(sm[:, h, :], sm[:, h, :], ACT.Exp, bias=top[:, h:h + 1],
                                             accum_out=den[:, h:h + 1]).then_inc(exped, 1)
                    for h in range(HEADS):
                        act.wait_ge(pt_ready, h + 1)
                        if h >= 2:
                            act.wait_ge(out_ready, h - 1)
                        nc.scalar.activation(pt[:, h % 2, :], ps_t[:, h % 2, :], ACT.Copy).then_inc(pt_taken, 1)


def rwkv_prepare(nc, s, layer, kmod1):
    z, rkv = s.z, s.rkv
    y, kka, kk = z[:, 0:4, :], z[:, 6:14, :], z[:, 14:18, :]
    kmod = (s.mix[:, 4:8, :], kmod1[:])

    with stage(nc, "conv_chain") as (block, chain):
        @block.vector
        def _(dve):
            with dve.Fori(0, 12) as b:
                link = Chain(dve, chain, b * 5)
                src, dst = z[:, bass.ds(b + Z_RKV, 1), :], rkv[:, bass.ds(b, 1), :]
                tap = [s.pv[:, bass.ds(b + (PV["conv"][0] + 12 * j), 1)] for j in range(3)]
                link(nc.vector.tensor_scalar(dst, src, tap[1], None, ALU.mult))
                for _, a, e in SEGMENTS:
                    link(nc.vector.scalar_tensor_tensor(dst[:, :, a + 1:e], src[:, :, a:e - 1], tap[0],
                                                        dst[:, :, a + 1:e], ALU.mult, ALU.add))
                    link(nc.vector.scalar_tensor_tensor(dst[:, :, a:e - 1], src[:, :, a + 1:e], tap[2],
                                                        dst[:, :, a:e - 1], ALU.mult, ALU.add))

    with ExitStack() as mem:
        ps = mem.enter_context(nc.psum_tensor("bonus_ps", [P, 8, 512], F32))
        with stage(nc, "bonus_ready", "bonus_summed", "bonus_chain") as (block, ready, summed, chain):
            @block.vector
            def _(dve):
                link = Chain(dve, chain)
                link(nc.vector.tensor_tensor(y, rkv[:, 0:4, :], rkv[:, 4:8, :], ALU.mult))
                nc.vector.tensor_tensor(y, y, bcast(s.pvs("r_k"), 2, T), ALU.mult).then_inc(ready, 1)
                nc.vector.tensor_tensor(kk, rkv[:, 4:8, :], bcast(s.pvs("k_k"), 2, T), ALU.mult)
                dve.wait_ge(summed, 1)
                nc.vector.tensor_copy(y.rearrange("p b (q n) -> p (b q) n", q=2), ps[:, :, 0:HALF])

            @block.tensor
            def _(pe):
                pe.wait_ge(ready, 1)
                for n in range(8):
                    last = nc.tensor.matmul(ps[:, n, 0:HALF], s.blk[:], y[:, n // 2, (n % 2) * HALF:(n % 2 + 1) * HALF],
                                            start=True, stop=True)
                last.then_inc(summed, 1)

    head_norm(nc, s, "kk", kk.rearrange("p b t -> p (b t)"), 4, HALF, 1.0, EPS, lambda dve, link: None)

    with ExitStack() as mem:
        rate_w = mem.enter_context(nc.sbuf_tensor("rate_w", [P, D_R], F32))
        half_a0 = mem.enter_context(nc.sbuf_tensor("half_a0", [P, 8], F32))
        one_ka = mem.enter_context(nc.sbuf_tensor("one_ka", [P, 4], F32))
        ps = mem.enter_context(nc.psum_tensor("rate_ps", [P, 4, 2, 512], F32))
        with stage(nc, "rate_loaded", "rate_done", "rate_tanh", "rate_small", "rate_chain") as \
                (block, loaded, done, tanhed, small, chain):
            @block.sync
            def _(sp):
                sp.dma_start(rate_w[:], s.d["a2"][bass.ds(layer, 1)].rearrange("a p n -> p (a n)")).then_inc(loaded, 16)

            @block.tensor
            def _(pe):
                pe.wait_ge(loaded, 16)
                for n in range(8):
                    d, b = n // 4, n % 4
                    if n >= 4:
                        pe.wait_ge(tanhed, n - 3)
                    for q in range(2):
                        last = nc.tensor.matmul(ps[:, n % 4, q, 0:HALF], rate_w[64 * d:64 * d + 64, b * P:(b + 1) * P],
                                                z[64 * d:64 * d + 64, Z_AD, q * HALF:(q + 1) * HALF],
                                                start=True, stop=True)
                    last.then_inc(done, 1)

            @block.scalar
            def _(act):
                act.wait_ge(small, 1)
                nc.scalar.activation(z[:, Z_WD, :], z[:, Z_WD, :], ACT.Tanh)
                for n in range(8):
                    act.wait_ge(done, n + 1)
                    nc.scalar.activation(kka[:, n, :].rearrange("p (q n) -> p q n", q=2), ps[:, n % 4, :, 0:HALF],
                                         ACT.Tanh, bias=half_a0[:, n:n + 1], scale=0.5).then_inc(tanhed, 1)

            @block.vector
            def _(dve):
                link = Chain(dve, chain)
                nc.vector.tensor_scalar(half_a0[:], s.pvs("a0"), 0.5, None, ALU.mult).then_inc(small, 1)
                link(nc.vector.tensor_scalar(one_ka[:], s.pvs("k_a"), -1.0, 1.0, ALU.mult, ALU.add))
                for d in range(2):
                    a = kka[:, 4 * d:4 * d + 4, :]
                    dve.wait_ge(tanhed, 4 * d + 4)
                    link(nc.vector.tensor_scalar(a, a, 0.5, 0.5, ALU.mult, ALU.add))
                    for b in range(4):
                        last = nc.vector.tensor_scalar(kmod[d][:, b, :], a[:, b, :], s.pvs("k_a")[:, b:b + 1],
                                                       one_ka[:, b:b + 1], ALU.mult, ALU.add)
                    link(last)
                    nc.vector.tensor_tensor(kmod[d], kmod[d], rkv[:, 4:8, :], ALU.mult)
                    link(nc.vector.tensor_tensor(a, a, kk, ALU.mult))
                link(nc.vector.tensor_tensor(rkv[:, 4:8, :], y, rkv[:, 8:12, :], ALU.mult))
                nc.vector.memset(y, 0.0)


def rwkv_tile(nc, s, w, layer, m, d):
    z = s.z
    y_all, kka, kk = z[:, 0:4, :], z[:, 6 + 4 * d:10 + 4 * d, :], z[:, 14:18, :]
    kmod = s.mix[:, 4:8, :] if d == 0 else w.kmod1[:]
    pair = w.ps[:].rearrange("p n c -> p (n c)")

    def bank(n):
        return w.ps[:, n, :]

    def bd_ps(n):
        return pair[:, n * 512:(n + 2) * 512].rearrange("p (j c) -> p j c", c=P)

    def half(ap, c):
        return ap[64 * c:64 * c + 64, :, 64 * c:64 * c + 64]

    def heads(ap):
        return ap.rearrange("p (b h v) -> p h b v", h=2, v=64)

    def head(ap, j):
        o = (j % 4) * P + (j // 4) * 64
        return ap[:, o:o + 64]

    def mask(k):
        return w.masks[:, d, k, :]

    def half_mask(k, c):
        return bcast(mask(k)[64 * c:64 * c + 64, :], 1, HEADS)

    halves = (slice(0, 4), slice(4, 8))

    x_bank, m_bank, mt_bank = (2, 4), (3, 5), (0, 6)

    def level_ps(banks, h):
        return bank(banks[h])[:, h * 256:h * 256 + 256].rearrange("p (j c) -> p j c", c=64)

    def level_count(lv, h):
        return 2 * lv + h if lv else 1

    tok = (m if d == 0 else m * -1 + (TILES - 1)) * P
    order = (0, 1) if d == 0 else (1, 0)
    t0, t1 = bass.ds(tok, P), None
    tag = "r%d_" % d
    names = ["init_in", "staged", "dec_done", "sw_raw", "sw_tanh", "sw_ready", "cum_done", "w_ready", "ab_ready",
             "rk_ready", "tr_done", "tr_taken", "prod_done", "prod_taken", "q1_done", "xz_ready", "pt_ready",
             "x_done", "x_ready", "mm_done", "m_ready", "z_done", "z_ready", "r_done", "r_ready", "y0_done",
             "y0_ready", "a_done", "a_ready", "b_done", "b_ready", "s_ready", "sp_done", "state_ready", "state_out",
             "dve_chain", "act_chain", "pool_chain", "mt_bd"]
    with stage(nc, *[tag + n for n in names]) as (block, *sems):
        e = dict(zip(names, sems))

        @block.sync
        def _(sp):
            sp.dma_start(w.init[:], s.d["state_in"][bass.ds(layer * (2 * TILES) + d * TILES + m, 1)]
                         .rearrange("a p n -> p (a n)")).then_inc(e["init_in"], 16)
            sp.wait_ge(e["state_ready"], 3)
            sp.dma_start(s.d["state_out"][bass.ds(layer * (2 * TILES) + d * TILES + m, 1)]
                         .rearrange("a p n -> p (a n)"), w.state[:, d].rearrange("p b v -> p (b v)")).then_inc(e["state_out"], 16)
            sp.wait_ge(e["state_out"], 16)

        @block.vector
        def _(dve):
            link = Chain(dve, e["dve_chain"])
            nc.vector.tensor_copy(w.kT[:, 0, :], z[:, Z_WD, t0])
            nc.vector.tensor_copy(w.rT[:], s.rkv[:, 8:12, t0]).then_inc(e["staged"], 1)
            dve.wait_ge(e["dec_done"], 1)
            nc.vector.tensor_tensor(w.sw[:], bank(0), s.w0_rows(d), ALU.add).then_inc(e["sw_raw"], 1)
            dve.wait_ge(e["sw_tanh"], 1)
            nc.vector.tensor_scalar(w.sw[:], w.sw[:], 0.5, 0.5, ALU.mult, ALU.add).then_inc(e["sw_ready"], 1)
            dve.wait_ge(e["init_in"], 16)
            nc.vector.scalar_tensor_tensor(w.state[:, d], w.state[:, d], w.keep[:, bass.ds(m + d * TILES, 1)],
                                           w.init[:].rearrange("p (b v) -> p b v", v=64), ALU.mult,
                                           ALU.add).then_inc(e["state_ready"], 1)
            dve.wait_ge(e["w_ready"], 3)
            nc.vector.tensor_tensor(w.aT[:], w.W[:, 2], kk[:, :, t0], ALU.mult)
            nc.vector.tensor_tensor(w.bT[:], w.W[:, 1], kka[:, :, t0], ALU.mult).then_inc(e["ab_ready"], 1)
            for c in range(2):
                last_tok = 64 * c + (63 if d == 0 else 0)
                link(nc.vector.tensor_copy(w.WC[:, c, :], w.W[:, 0, :, last_tok]))

            def masked(n, ps_n, dst, k):
                dve.wait_ge(e["prod_done"], n)
                for c in range(2):
                    last = nc.vector.tensor_tensor(half(dst[:], c), half(bd_ps(ps_n), c), half_mask(k, c), ALU.mult)
                last.then_inc(e["prod_taken"], 1)

            masked(1, 4, w.LT, 0)
            masked(2, 6, w.PT0, 0)
            dve.wait_ge(e["prod_done"], 3)
            for c in range(2):
                ins = nc.vector.tensor_tensor(w.M[64 * c:64 * c + 64], half(bd_ps(2), c), half_mask(3, c), ALU.mult)
                if c == 1:
                    ins.then_inc(e["prod_taken"], 1)
            dve.wait_ge(e["prod_taken"], 3)
            link(nc.vector.tensor_tensor(w.M[:], w.M[:], bcast(w.ident2[:], 1, HEADS), ALU.add))
            for c in range(2):
                last = nc.vector.tensor_tensor(w.MTc[64 * c:64 * c + 64], half(w.LT[:], c), half_mask(4, c), ALU.mult)
            link(last)
            nc.vector.tensor_tensor(w.MTc[:], w.MTc[:], bcast(w.ident2[:], 1, HEADS), ALU.add).then_inc(e["m_ready"], 1)
            masked(4, 4, w.FT, 1)
            masked(5, 6, w.GT, 2)
            for lv in range(1, LEVELS):
                for h, js in enumerate(halves):
                    dve.wait_ge(e["mm_done"], 2 * (lv - 1) + h + 1)
                    if lv < LEVELS - 1:
                        nc.vector.tensor_tensor(w.M[:, js], w.M[:, js], level_ps(m_bank, h),
                                                ALU.subtract)
                    nc.vector.tensor_tensor(w.MTc[:, js], w.MTc[:, js], level_ps(mt_bank, h),
                                            ALU.subtract).then_inc(e["m_ready"], 1)
            for h, js in enumerate(halves):
                dve.wait_ge(e["z_done"], h + 1)
                nc.vector.tensor_copy(w.Z[:, js], bd_ps(4)[:, js]).then_inc(e["z_ready"], 1)
            dve.wait_ge(e["r_done"], 1)
            nc.vector.tensor_tensor(w.kT[:], bank(6).rearrange("p (b c) -> p b c", c=P), w.rT[:],
                                    ALU.add).then_inc(e["r_ready"], 1)
            dve.wait_ge(e["b_done"], 1)
            link(nc.vector.tensor_copy(w.B[:], bank(2)))
            for n, c in enumerate(order):
                dve.wait_ge(e["state_ready"], n + 1)
                for h in range(2):
                    last = nc.vector.tensor_copy(w.S_bd[64 * h:64 * h + 64, :, 64 * h:64 * h + 64],
                                                 w.state[64 * h:64 * h + 64, d, :, :])
                last.then_inc(e["s_ready"], 1)
                dve.wait_ge(e["sp_done"], 2 * n + 1)
                link(nc.vector.tensor_tensor(w.state[:, d], bank(3)[:, 0:256].rearrange("p (b v) -> p b v", v=64),
                                             w.state[:, d], ALU.add))
                link(nc.vector.tensor_tensor(w.state[:, d], w.state[:, d],
                                             w.B[:].rearrange("p (c b v) -> p c b v", c=2, v=64)[:, c], ALU.add))
                nc.vector.tensor_tensor(w.state[:, d], w.state[:, d], bcast(w.WC[:, c, :], 2, 64),
                                        ALU.mult).then_inc(e["state_ready"], 1)
                dve.wait_ge(e["sp_done"], 2 * n + 2)
            dve.wait_ge(e["y0_ready"], 1)
            link(nc.vector.tensor_tensor(w.Y0[:], w.Y0[:], bank(0).rearrange("p (b c) -> p b c", c=P), ALU.add))
            nc.vector.tensor_tensor(y_all[:, :, t0], y_all[:, :, t0], w.Y0[:], ALU.add)

        @block.gpsimd
        def _(pool):
            pool.wait_ge(e["w_ready"], 3)
            pool.wait_ge(e["tr_done"], 1)
            nc.gpsimd.tensor_tensor(w.rT[:], w.W[:, 0], s.rkv[:, 0:4, t0], ALU.mult).then_inc(e["rk_ready"], 1)
            nc.gpsimd.tensor_tensor(w.kT[:], w.W[:, 1], kmod[:, :, t0], ALU.mult).then_inc(e["rk_ready"], 1)
            for lv in range(1, LEVELS):
                dst = (w.PT1, w.PT0)[(lv - 1) % 2]
                if lv == 1:
                    pool.wait_ge(e["prod_taken"], 1)
                elif lv == 2:
                    pool.wait_ge(e["q1_done"], 1)
                else:
                    pool.wait_ge(e["x_done"], 2 * (lv - 2))
                nc.gpsimd.tensor_tensor(dst[:].rearrange("p j (c t) -> p (j c) t", c=2),
                                        w.LT[:].rearrange("p j (c t) -> p (j c) t", c=2),
                                        bcast(mask(4 + lv), 1, 2 * HEADS), ALU.mult).then_inc(e["pt_ready"], 1)

        @block.scalar
        def _(act):
            link = Chain(act, e["act_chain"])
            act.wait_ge(e["sw_raw"], 1)
            nc.scalar.activation(w.sw[:], w.sw[:], ACT.Tanh, scale=0.5).then_inc(e["sw_tanh"], 1)
            act.wait_ge(e["tr_done"], 1)
            nc.scalar.activation(w.V[:], bank(1), ACT.Copy).then_inc(e["tr_taken"], 1)
            act.wait_ge(e["cum_done"], 1)
            cum = pair[:, 1024:2048].rearrange("p (b x t) -> p b x t", x=2, t=P)
            nc.scalar.activation(w.W[:, 2], cum[:, :, 1, :], ACT.Exp, scale=-DECAY).then_inc(e["w_ready"], 1)
            nc.scalar.activation(w.W[:, 1], cum[:, :, 0, :], ACT.Exp, scale=DECAY).then_inc(e["w_ready"], 1)
            nc.scalar.activation(w.W[:, 0], cum[:, :, 0, :], ACT.Exp, scale=-DECAY).then_inc(e["w_ready"], 1)

            def tokens_bd(dst, ps_n, sign):
                src = heads(bank(ps_n))
                for c in range(2):
                    for h in range(2):
                        last = nc.scalar.activation(dst[64 * c:64 * c + 64, 4 * h:4 * h + 4, 64 * c:64 * c + 64],
                                                    src[64 * c:64 * c + 64, h], ACT.Copy, scale=sign)
                return last

            act.wait_ge(e["tr_done"], 2)
            tokens_bd(w.nb, 1, -1.0).then_inc(e["tr_taken"], 1)
            act.wait_ge(e["tr_done"], 3)
            act.wait_ge(e["rk_ready"], 2)
            act.wait_ge(e["dve_chain"], 2)
            for h in range(2):
                last = nc.scalar.activation(w.XZ[:, 4 * h:4 * h + 4, 0:64], heads(bank(0))[:, h], ACT.Copy)
            last.then_inc(e["tr_taken"], 1)
            act.wait_ge(e["tr_done"], 4)
            tokens_bd(w.kt, 1, 1.0).then_inc(e["tr_taken"], 1)
            act.wait_ge(e["m_ready"], 1)
            for c in range(2):
                last = nc.scalar.activation(half(w.MT[:], c), w.MTc[64 * c:64 * c + 64], ACT.Copy)
            last.then_inc(e["mt_bd"], 1)
            act.wait_ge(e["q1_done"], 1)
            nc.scalar.activation(w.XZ[:, :, 64:128], bank(1).rearrange("p (j v) -> p j v", v=64),
                                 ACT.Copy).then_inc(e["xz_ready"], 1)
            for lv in range(1, LEVELS):
                for h, js in enumerate(halves):
                    act.wait_ge(e["x_done"], 2 * (lv - 1) + h + 1)
                    src = level_ps(x_bank, h)
                    if lv < LEVELS - 1:
                        nc.scalar.activation(w.Xc[:, js], src, ACT.Copy)
                    for c in range(2):
                        last = nc.scalar.activation(half(w.X[:, js], c), src[64 * c:64 * c + 64], ACT.Copy)
                    last.then_inc(e["x_ready"], 1)
                for h, js in enumerate(halves):
                    act.wait_ge(e["m_ready"], level_count(lv, h))
                    for c in range(2):
                        last = nc.scalar.activation(half(w.MT[:, js], c), w.MTc[64 * c:64 * c + 64, js], ACT.Copy)
                    last.then_inc(e["mt_bd"], 1)
            act.wait_ge(e["a_done"], 1)
            at = bank(1).rearrange("p (b c k) -> p c b k", c=2, k=64)
            for h in range(2):
                for c in range(2):
                    last = nc.scalar.activation(w.X[:].rearrange("p (c b) k -> p c b k", c=2)
                                                [64 * h:64 * h + 64, c, :, 64 * h:64 * h + 64],
                                                at[64 * h:64 * h + 64, c], ACT.Copy)
            last.then_inc(e["a_ready"], 1)
            act.wait_ge(e["y0_done"], 1)
            nc.scalar.activation(w.Y0[:], bank(7).rearrange("p (b c) -> p b c", c=P), ACT.Copy).then_inc(e["y0_ready"], 1)

        @block.tensor
        def _(pe):
            mm, tr = nc.tensor.matmul, nc.tensor.transpose
            pe.wait_ge(e["staged"], 1)
            mm(bank(0), w.kT[64 * d:64 * d + 64, 0, :], w.w2[64 * d:64 * d + 64, :], start=True,
               stop=True).then_inc(e["dec_done"], 1)
            for b in range(RB):
                last = tr(bank(1)[:, b * P:(b + 1) * P], w.rT[:, b, :], s.ident[:])
            last.then_inc(e["tr_done"], 1)
            pe.wait_ge(e["sw_ready"], 1)
            for b in range(RB):
                last = mm(pair[:, 1024 + b * 256:1280 + b * 256], w.sw[:, b * P:(b + 1) * P], w.tri[:, d, :],
                          start=True, stop=True)
            last.then_inc(e["cum_done"], 1)

            def product(ps_n, left, right):
                for j in range(HEADS):
                    f = slice(64 * (j // 4), 64 * (j // 4) + 64)
                    last = mm(bd_ps(ps_n)[:, j, :], left[f, j % 4, :], right[f, j % 4, :], start=True, stop=True)
                last.then_inc(e["prod_done"], 1)

            def to_tokens(ps_n, src):
                for b in range(RB):
                    last = tr(bank(ps_n)[:, b * P:(b + 1) * P], src[:, b, :], s.ident[:])
                last.then_inc(e["tr_done"], 1)

            pe.wait_ge(e["ab_ready"], 1)
            product(4, w.bT, w.aT)
            pe.wait_ge(e["tr_taken"], 1)
            to_tokens(1, w.bT)
            to_tokens(0, w.aT)
            pe.wait_ge(e["rk_ready"], 2)
            product(6, w.kT, w.aT)
            product(2, w.aT, w.bT)
            pe.wait_ge(e["tr_taken"], 2)
            to_tokens(1, w.kT)
            pe.wait_ge(e["prod_taken"], 1)
            product(4, w.bT, w.rT)
            pe.wait_ge(e["prod_taken"], 2)
            product(6, w.kT, w.rT)
            pe.wait_ge(e["tr_taken"], 4)
            for j in range(HEADS):
                last = mm(bank(1)[:, j * 64:(j + 1) * 64], w.PT0[:, j, :], head(w.V[:], j), start=True, stop=True)
            last.then_inc(e["q1_done"], 1)
            for lv in range(1, LEVELS):
                pt = (w.PT1, w.PT0)[(lv - 1) % 2]
                pe.wait_ge(e["pt_ready"], lv)
                for h in range(2):
                    pe.wait_ge(e["m_ready"], level_count(lv - 1, h))
                    if lv == 1 and h == 1:
                        pe.wait_ge(e["prod_taken"], 5)
                    for j in range(4 * h, 4 * h + 4):
                        last = mm(bank(x_bank[h])[:, j * 64:(j + 1) * 64], pt[:, j, :], w.M[:, j, :], start=True, stop=True)
                    last.then_inc(e["x_done"], 1)
                for h in range(2):
                    pe.wait_ge(e["mt_bd"], level_count(lv - 1, h))
                    pe.wait_ge(e["x_ready"], 2 * (lv - 1) + h + 1)
                    for j in range(4 * h, 4 * h + 4):
                        if lv < LEVELS - 1:
                            mm(bank(m_bank[h])[:, j * 64:(j + 1) * 64], w.MT[:, j, :], w.Xc[:, j, :], start=True, stop=True)
                        last = mm(bank(mt_bank[h])[:, j * 64:(j + 1) * 64], w.X[:, j, :], w.MTc[:, j, :],
                                  start=True, stop=True)
                    last.then_inc(e["mm_done"], 1)
            pe.wait_ge(e["xz_ready"], 1)
            pe.wait_ge(e["prod_taken"], 5)
            for h in range(2):
                pe.wait_ge(e["mt_bd"], level_count(LEVELS - 1, h))
                for j in range(4 * h, 4 * h + 4):
                    last = mm(bd_ps(4)[:, j, :], w.MT[:, j, :], w.XZ[:, j, :], start=True, stop=True)
                last.then_inc(e["z_done"], 1)

            def rows(j):
                return slice(64 * (j // 4), 64 * (j // 4) + 64)

            for j in range(HEADS):
                if j % 4 == 0:
                    pe.wait_ge(e["z_ready"], j // 4 + 1)
                b = j % 4
                last = mm(bank(6)[rows(j), b * P:(b + 1) * P], w.Z[:, j, 0:64], w.FT[:, j, :], start=True, stop=True)
            last.then_inc(e["r_done"], 1)
            for j in range(HEADS):
                b = j % 4
                last = mm(bank(1)[rows(j), b * P:(b + 1) * P], w.Z[:, j, 0:64], w.nb[:, j, :], start=True, stop=True)
            last.then_inc(e["a_done"], 1)
            for j in range(HEADS):
                for c in range(2):
                    o = bank(2)[rows(j), (c * 4 + j % 4) * 64:(c * 4 + j % 4 + 1) * 64]
                    mm(o, w.kt[:, j, 64 * c:64 * c + 64], head(w.V[:], j), start=True, stop=False)
                    last = mm(o, w.nb[:, j, 64 * c:64 * c + 64], w.Z[:, j, 64:128], start=False, stop=True)
            last.then_inc(e["b_done"], 1)
            for j in range(HEADS):
                o = bank(7)[rows(j), (j % 4) * P:(j % 4 + 1) * P]
                mm(o, head(w.V[:], j), w.GT[:, j, :], start=True, stop=False)
                last = mm(o, w.Z[:, j, 64:128], w.FT[:, j, :], start=False, stop=True)
            last.then_inc(e["y0_done"], 1)
            pe.wait_ge(e["a_ready"], 1)
            pe.wait_ge(e["r_ready"], 1)
            for n, c in enumerate(order):
                pe.wait_ge(e["s_ready"], n + 1)
                for b in range(RB):
                    last = mm(bank(3)[:, b * 64:(b + 1) * 64], w.X[:, c * 4 + b, :], w.state[:, d, b, :],
                              start=True, stop=True)
                last.then_inc(e["sp_done"], 1)
                for b in range(RB):
                    last = mm(bank(0)[:, b * P + 64 * c:b * P + 64 * c + 64], w.S_bd[:, b, :],
                              w.kT[:, b, 64 * c:64 * c + 64], start=True, stop=True)
                last.then_inc(e["sp_done"], 1)


def rwkv(nc, s, layer):
    with ExitStack() as mem:
        def sb(name, *shape):
            return mem.enter_context(nc.sbuf_tensor("rw_" + name, [P, *shape], F32))

        s.rkv = sb("rkv", 12, T)
        kmod1 = sb("kmod1", 4, T)
        rwkv_prepare(nc, s, layer, kmod1)
        with ExitStack() as work:
            def wb(name, *shape):
                return work.enter_context(nc.sbuf_tensor("rw_" + name, [P, *shape], F32))

            w = Names()
            w.kmod1 = kmod1
            w.masks, w.tri, w.ident2 = wb("masks", 2, 10, 64), wb("tri", 2, 2 * P), wb("ident2", 64)
            w.keep, w.w2, w.init, w.state = wb("keep", 2 * TILES), wb("w2", D_R), wb("init", 256), wb("state", 2, RB, 64)
            w.sw = wb("sw", D_R)
            w.MTc = w.sw[:].rearrange("p (j c) -> p j c", c=64)
            W = wb("W", 3 * D_R)
            w.W = W[:].rearrange("p (n b t) -> p n b t", n=3, t=P)
            w.XZ = W[:, 0:1024].rearrange("p (j c) -> p j c", c=P)
            w.Xc = W[:, 1024:1536].rearrange("p (j c) -> p j c", c=64)
            w.Y0 = W[:, 1024:1536].rearrange("p (b t) -> p b t", t=P)
            ab = wb("ab", 2 * D_R)
            w.aT = ab[:, 0:D_R].rearrange("p (b t) -> p b t", t=P)
            w.bT = ab[:, D_R:].rearrange("p (b t) -> p b t", t=P)
            w.Z = ab[:].rearrange("p (j c) -> p j c", c=P)
            w.rT, w.kT, w.V = wb("rT", RB, P), wb("kT", RB, P), wb("V", D_R)
            bd = [wb(n, HEADS, P) for n in ("nb", "kt", "LT", "PT0", "PT1", "FT", "GT", "MT", "X")]
            w.nb, w.kt, w.LT, w.PT0, w.PT1, w.FT, w.GT, w.MT, w.X = bd
            w.M = wb("M", HEADS, 64)
            w.B = w.M[:].rearrange("p j c -> p (j c)")
            w.S_bd, w.WC = wb("S_bd", RB, P), wb("WC", 2, RB)
            w.ps = work.enter_context(nc.psum_tensor("rw_ps", [P, 8, 512], F32))
            s.w0_rows = lambda d: s.z[:, 4:6, :].rearrange("p b t -> p (b t)")[:, d * D_R:(d + 1) * D_R]
            with stage(nc, "rw_loaded") as (block, loaded):
                @block.sync
                def _(sp):
                    for dst, src in ((w.masks, s.d["r_masks"]), (w.tri, s.d["tri"]), (w.ident2, s.d["ident2"]),
                                     (w.keep, s.d["keep"])):
                        sp.dma_start(dst[:], src).then_inc(loaded, 16)
                    sp.dma_start(w.w2[:], s.d["w2"][bass.ds(layer, 1)].rearrange("a p n -> p (a n)")).then_inc(loaded, 16)
                    sp.dma_start(s.z[:, 4:6, :].rearrange("p b t -> p (b t)")[:, 0:2 * D_R],
                                 s.d["w0"][bass.ds(layer, 1)].rearrange("a p n -> p (a n)")).then_inc(loaded, 16)
                    sp.wait_ge(loaded, 96)

                @block.vector
                def _(dve):
                    for buffer in (*bd, w.S_bd, w.state):
                        nc.vector.memset(buffer[:], 0.0)
            with nc.Fori(0, TILES) as m:
                for d in range(2):
                    rwkv_tile(nc, s, w, layer, m, d)
        rwkv_finish(nc, s, layer)


def rwkv_finish(nc, s, layer):
    y, bonus = s.z[:, 0:4, :], s.rkv[:, 4:8, :]

    def pieces(ap, n):
        return ap[:, n // 2, (n % 2) * HALF:(n % 2 + 1) * HALF]

    with ExitStack() as mem:
        ps = mem.enter_context(nc.psum_tensor("mean_ps", [P, 8, 512], F32))
        with stage(nc, "mean_done") as (block, done):
            @block.tensor
            def _(pe):
                for n in range(8):
                    last = nc.tensor.matmul(ps[:, n, 0:HALF], s.blk[:], pieces(y, n), start=True, stop=True)
                last.then_inc(done, 1)

            @block.vector
            def _(dve):
                dve.wait_ge(done, 1)
                yq = y.rearrange("p b (q n) -> p (b q) n", q=2)
                nc.vector.scalar_tensor_tensor(yq, ps[:, :, 0:HALF], -1.0 / HD, yq, ALU.mult, ALU.add)

    def affine(dve, link):
        for b in range(RB):
            last = nc.vector.tensor_scalar(y[:, b, :], y[:, b, :], s.pvs("ln_g")[:, b:b + 1],
                                           s.pvs("ln_b")[:, b:b + 1], ALU.mult, ALU.add)
        link(last)
        link(nc.vector.tensor_tensor(y, y, bonus, ALU.add))

    head_norm(nc, s, "gn", y.rearrange("p b t -> p (b t)"), 4, HALF, 1.0 / HD, GN_EPS, affine)

    with ExitStack() as mem:
        g2 = mem.enter_context(nc.sbuf_tensor("gate_w", [P, D_R], F32))
        ps = mem.enter_context(nc.psum_tensor("gate_ps", [P, 8, 512], F32))
        with stage(nc, "gate_loaded", "gate_tanh", "gate_ready", "gate_done") as (block, loaded, tanhed, ready, done):
            gd = s.z[:, Z_GD, :]

            @block.sync
            def _(sp):
                sp.dma_start(g2[:], s.d["g2"][bass.ds(layer, 1)].rearrange("a p n -> p (a n)")).then_inc(loaded, 16)

            @block.scalar
            def _(act):
                nc.scalar.activation(gd, gd, ACT.Tanh, scale=0.5).then_inc(tanhed, 1)

            @block.tensor
            def _(pe):
                pe.wait_ge(loaded, 16)
                pe.wait_ge(ready, 1)
                for n in range(8):
                    last = nc.tensor.matmul(ps[:, n, 0:HALF], g2[:, (n // 2) * P:(n // 2 + 1) * P],
                                            gd[:, (n % 2) * HALF:(n % 2 + 1) * HALF], start=True, stop=True)
                last.then_inc(done, 1)

            @block.vector
            def _(dve):
                dve.wait_ge(tanhed, 1)
                nc.vector.tensor_scalar(gd, gd, 0.5, 0.5, ALU.mult, ALU.add).then_inc(ready, 1)
                dve.wait_ge(done, 1)
                nc.vector.tensor_tensor(s.mix[:, 4:8, :].rearrange("p b (q n) -> p (b q) n", q=2),
                                        ps[:, :, 0:HALF], y.rearrange("p b (q n) -> p (b q) n", q=2), ALU.mult)


def split_mix(nc, s, hi, lo):
    with stage(nc, "mix_hi") as (block, hi_ready):
        @block.scalar
        def _(act):
            for b in range(KB):
                nc.scalar.activation(hi[:, b], s.mix[:, b], ACT.Copy).then_inc(hi_ready, 1)

        @block.vector
        def _(dve):
            for b in range(KB):
                dve.wait_ge(hi_ready, b + 1)
                nc.vector.tensor_tensor(lo[:, b], s.mix[:, b], hi[:, b].bitcast(F32), ALU.subtract)


def output_projection(nc, s, layer, hi, lo):
    def evacuate(act, i, u, ps):
        return nc.scalar.activation(s.mix[:, bass.ds(i * 2 + u, 1), :].rearrange("p a (q n) -> p (a q) n", q=2),
                                    ps[:, :, 0:HALF], ACT.Copy)
    project(nc, s, "out", layer, IN_BLOCKS, OUT_BLOCKS, 2, hi, lo, evacuate)
    add_gated(nc, s, "mixed", s.mix, 2 * KB)


def add_gated(nc, s, name, y, gate):
    with stage(nc, name + "_chain") as (block, chain):
        @block.vector
        def _(dve):
            for b in range(KB):
                for c, lo, hi in SEGMENTS:
                    nc.vector.scalar_tensor_tensor(s.x[:, b, lo:hi], y[:, b, lo:hi], s.mod[:, gate + b, c:c + 1],
                                                   s.x[:, b, lo:hi], ALU.mult, ALU.add)


def query_scores(nc, s, layer, hi, lo, best, best_f):
    with ExitStack() as mem:
        q = mem.enter_context(nc.sbuf_tensor("q_block", [P, 2, T], F32))
        keys = mem.enter_context(nc.sbuf_tensor("sub_keys", [P, 2, N_KEYS], F32))
        sc = mem.enter_context(nc.sbuf_tensor("sc", [P, TILES, N_KEYS], F32))
        val = mem.enter_context(nc.sbuf_tensor("sc_val", [P, TILES, TOPK], F32))
        idx = mem.enter_context(nc.sbuf_tensor("sc_idx", [P, TILES, TOPK], U32))
        idle = mem.enter_context(nc.sbuf_tensor("sc_idle", [P, 1], F32))
        ps = mem.enter_context(nc.psum_tensor("score_ps", [P, 2, 8, N_KEYS], F32))
        with stage(nc, "keys_loaded") as (block, loaded):
            @block.sync
            def _(sp):
                sp.dma_start(keys[:], s.d["sub_keys"][bass.ds(layer, 1)].rearrange("a p c n -> p (a c) n")).then_inc(loaded, 16)
                sp.wait_ge(loaded, 16)

        def evacuate(act, i, u, block_ps, sc_done, sc_taken, chain):
            act.wait_ge(sc_done, i * 2 + u + 1)
            return nc.scalar.activation(q[:, u].rearrange("p (q n) -> p q n", q=2), block_ps[:, :, 0:HALF], ACT.Copy)

        def multiply(pe, i, taken, sc_done, sc_taken, chain):
            for u in range(2):
                pe.wait_ge(taken, i * 2 + 2 + u + 1)
                pe.wait_ge(sc_taken, i * 2 + u + 1)
                for m in range(TILES):
                    last = nc.tensor.matmul(ps[:, u, m, :], q[:, u, m * P:(m + 1) * P], keys[:, u, :],
                                            start=True, stop=True)
                last.then_inc(sc_done, 1)

        def take(dve, i, sc_done, sc_taken, chain):
            v, counted = nc.vector, Chain(dve, chain, i * 8)

            def link(ins=None):
                if ins is not None:
                    counted(ins)
                v.memset(idle[:], 0.0)

            for u in range(2):
                dve.wait_ge(sc_done, i * 2 + 2 + u + 1)
                v.tensor_copy(sc[:], ps[:, u, 0:TILES, :]).then_inc(sc_taken, 1)
                dve.wait_ge(sc_taken, i * 2 + 2 + u + 1)
                link()
                for m in range(TILES):
                    last = v.max(val[:, m, 0:8], sc[:, m, :])
                link(last)
                for m in range(TILES):
                    v.max_index(idx[:, m, 0:8], val[:, m, 0:8], sc[:, m, :])
                    last = v.match_replace(sc[:, m, :], val[:, m, 0:8], sc[:, m, :], MIN_F32)
                link(last)
                for m in range(TILES):
                    last = v.max(val[:, m, 8:16], sc[:, m, :])
                link(last)
                for m in range(TILES):
                    last = v.max_index(idx[:, m, 8:16], val[:, m, 8:16], sc[:, m, :])
                link(last)
                row = bass.ds(i * 2 + u, 1)
                v.tensor_copy(best[:, :, row, :].rearrange("p m a k -> p m (a k)"), val[:])
                v.tensor_copy(best_f[:, :, row, :].rearrange("p m a k -> p m (a k)"), idx[:])

        project(nc, s, "qry", layer, IN_BLOCKS + OUT_BLOCKS, Q_BLOCKS, 2, hi, lo, evacuate,
                (multiply, take))


def retrieve(nc, s, best, best_f):
    H, K = HEADS, TOPK
    HH = H // 2
    B, S = 4, 4
    CHUNKS = P // (B * S)
    with ExitStack() as mem:
        def sb(name, shape, dt=F32):
            return mem.enter_context(nc.sbuf_tensor("tk_" + name, shape, dt))

        iota = sb("iota", [P, P])
        iota_b = sb("iota_b", [P, P], BF16)
        cand, hot = sb("cand", [P, H, K * K]), sb("hot", [P, 2, H, K, K], BF16)
        top, top_i = sb("top", [P, H, K]), sb("top_i", [P, H, K], U32)
        slot_i, slot = sb("slot_i", [P, 2, H, K], U32), sb("slot", [P, 2, H, K], BF16)
        ghk = sb("ghk", [P, 3, H * K])
        den = sb("den", [P, H])
        num_hk, g_hk = sb("num_hk", [P, 2, P], BF16), sb("g_hk", [P, P])
        one_hot = sb("one_hot", [P, S, 2, B, P], BF16)
        on_j, on_i = sb("on_j", [P, S, B, P]), sb("on_i", [P, S, B, P])
        grid = sb("grid", [P, 2, P, P // 2])
        ps_t = mem.enter_context(nc.psum_tensor("tk_ps_t", [P, 3, P], F32))
        ps_g = mem.enter_context(nc.psum_tensor("tk_ps_g", [P, S, B, P], F32))
        stored = [nc.alloc_semaphore("tk_stored%d" % h, num=FIRST_SEM - 2 + h) for h in range(2)]
        with stage(nc, "iota_in") as (block, iota_in):
            @block.sync
            def _(sp):
                sp.dma_start(iota[:], s.d["iota"]).then_inc(iota_in, 16)

            @block.vector
            def _(dve):
                dve.wait_ge(iota_in, 16)
                nc.vector.tensor_copy(iota_b[:], iota[:])

        def step(part, nxt, cur):
            with stage(nc, "tk_chain_" + part, "tk_exp_in", "tk_exp", "tk_turned", "tk_chosen", "tk_on_i", "tk_on_j",
                       "tk_grid", "tk_taken", "tk_hot") as                     (block, chain, exp_in, exped, turned, chosen, oni_ready, onj_ready, grid_ps, taken, hot_ready):
                @block.vector
                def _(dve):
                    v, link = nc.vector, Chain(dve, chain)
                    g = ghk[:, 2, :].rearrange("p (h k) -> p h k", k=K)

                    def candidates():
                        pair = best[:, bass.ds(nxt, 1), :, :].rearrange("p m (h c) k -> p (m h) c k", c=2)
                        link(v.tensor_tensor(cand[:].rearrange("p h (a b) -> p h a b", a=K),
                                             bcast(pair[:, :, 0, :], 3, K), bcast(pair[:, :, 1, :], 2, K), ALU.add))

                    def top16(heads):
                        for h in heads:
                            last = v.max(top[:, h, 0:8], cand[:, h, :])
                        link(last)
                        for h in heads:
                            v.max_index(top_i[:, h, 0:8], top[:, h, 0:8], cand[:, h, :])
                            last = v.match_replace(cand[:, h, :], top[:, h, 0:8], cand[:, h, :], MIN_F32)
                        link(last)
                        for h in heads:
                            last = v.max(top[:, h, 8:16], cand[:, h, :])
                        link(last)
                        for h in heads:
                            last = v.max_index(top_i[:, h, 8:16], top[:, h, 8:16], cand[:, h, :])
                        link(last)

                    def ranks():
                        v.tensor_scalar(slot_i[:, 0], top_i[:], 4, None, ALU.logical_shift_right)
                        link(v.tensor_scalar(slot_i[:, 1], top_i[:], K - 1, None, ALU.bitwise_and))
                        link(v.tensor_copy(slot[:], slot_i[:]))

                    def numbers(c):
                        which = best_f[:, bass.ds(nxt, 1), :, :].rearrange("p m (h c) k -> p (m h) c k", c=2)[:, :, c, :]
                        link(v.tensor_tensor(hot[:, c], bcast(slot[:, c], 3, K),
                                             bcast(bcast(iota_b[:, 0:K], 1, K), 1, H), ALU.is_equal))
                        link(v.tensor_tensor(hot[:, c], hot[:, c], bcast(which, 2, K), ALU.mult))
                        link(v.tensor_reduce(ghk[:, c, :].rearrange("p (h k) -> p h k", k=K), hot[:, c], AX.X, ALU.add))

                    if nxt is not None:
                        candidates()
                    for c in range(CHUNKS):
                        if cur is not None:
                            with dve.Fori(0, 2) as j:
                                for u in range(2):
                                    dve.wait_ge(oni_ready, j * 2 + (c * S + u + 1))
                                    dve.wait_ge(onj_ready, j * 2 + (c * S + u + 1))
                                    tok = bass.ds(j * (2 * B) + (c * S + u) * B, B)
                                    v.tensor_tensor(one_hot[:, bass.ds(j * 2 + u, 1)].rearrange("p a n t k -> p (a n) t k"),
                                                    bcast(bcast(iota_b[:], 1, B), 1, 2), bcast(num_hk[:, :, tok], 3, P),
                                                    ALU.is_equal).then_inc(hot_ready, 1)
                        if nxt is None:
                            continue
                        if c < 4:
                            top16((2 * c, 2 * c + 1))
                        if c == 3:
                            v.tensor_tensor(g, top[:], top[:, :, 0:1].broadcast_to([P, H, K]),
                                            ALU.subtract).then_inc(exp_in, 1)
                            ranks()
                        if c == 4:
                            numbers(0)
                        if c == 5:
                            numbers(1)
                        if c == 6:
                            dve.wait_ge(exped, 1)
                            link(v.tensor_reduce(den[:], g, AX.X, ALU.add))
                            link(v.reciprocal(den[:], den[:]))
                            v.tensor_tensor(g, g, bcast(den[:], 2, K), ALU.mult).then_inc(chosen, 1)
                    if nxt is not None:
                        if cur is not None:
                            dve.wait_ge(hot_ready, P // B)
                            dve.wait_ge(oni_ready, S + P // B)
                        dve.wait_ge(turned, 1)
                        v.tensor_copy(num_hk[:], ps_t[:, 0:2])
                        link(v.tensor_copy(g_hk[:], ps_t[:, 2]))

                @block.gpsimd
                def _(pool):
                    if cur is not None:
                        pool.sem_inc(oni_ready, S)
                        with pool.Fori(0, CHUNKS) as i:
                            for u in range(S):
                                pool.wait_ge(hot_ready, i * S + u + 1)
                                pool.wait_ge(grid_ps, i * S + u + 1)
                                nc.gpsimd.tensor_tensor(on_i[:, u], one_hot[:, u, 0],
                                                        bcast(g_hk[:, bass.ds(i * (S * B) + u * B, B)], 2, P),
                                                        ALU.mult).then_inc(oni_ready, 1)

                @block.scalar
                def _(act):
                    def weights():
                        act.wait_ge(exp_in, 1)
                        nc.scalar.activation(ghk[:, 2, :], ghk[:, 2, :], ACT.Exp).then_inc(exped, 1)

                    def widen(n, u):
                        act.wait_ge(hot_ready, n + 1)
                        act.wait_ge(grid_ps, n + 1)
                        nc.scalar.activation(on_j[:, u], one_hot[:, u, 1], ACT.Copy).then_inc(onj_ready, 1)

                    if cur is not None:
                        act.sem_inc(taken, S)
                        act.sem_inc(onj_ready, S)
                        for u in range(S - 1):
                            widen(u, u)
                        for half in range(2):
                            if half == 1 and nxt is not None:
                                weights()
                            act.wait_ge(stored[half], cur * 16 + 1)
                            first = half * (CHUNKS // 2) * S
                            n_chunks = CHUNKS // 2 - half

                            def take(i, u):
                                act.wait_ge(grid_ps, i * S + (first + S + u + 1))
                                out = grid[:, half, :, bass.ds(i * (S * B) + u * B, B)].rearrange("p i t -> p t i")
                                nc.scalar.activation(out, ps_g[:, u], ACT.Copy).then_inc(taken, 1)

                            with act.Fori(0, n_chunks) as i:
                                for u in range(S):
                                    widen(i * S + (first + u + S - 1), (u + S - 1) % S)
                                    take(i, u)
                        widen(P // B - 1, S - 1)
                        for u in range(S):
                            take(n_chunks, u)
                    else:
                        for half in range(2):
                            act.sem_inc(stored[half], 1)
                        weights()

                @block.tensor
                def _(pe):
                    if cur is not None:
                        pe.sem_inc(grid_ps, S)
                        with pe.Fori(0, CHUNKS) as i:
                            for u in range(S):
                                pe.wait_ge(oni_ready, i * S + S + u + 1)
                                pe.wait_ge(onj_ready, i * S + S + u + 1)
                                pe.wait_ge(taken, i * S + u + 1)
                                for t in range(B):
                                    last = nc.tensor.matmul(ps_g[:, u, t, :], on_j[:, u, t, :], on_i[:, u, t, :],
                                                            start=True, stop=True)
                                last.then_inc(grid_ps, 1)
                    if nxt is not None:
                        pe.wait_ge(chosen, 1)
                        for n in range(3):
                            last = nc.tensor.transpose(ps_t[:, n, :], ghk[:, n, :], s.ident[:])
                        last.then_inc(turned, 1)

                @block.sync
                def _(sp):
                    if cur is not None:
                        for half in range(2):
                            sp.wait_ge(taken, S + (half + 1) * (CHUNKS // 2) * S)
                            sp.dma_start(s.d["grid"][bass.ds(cur * 2 + half, 1)].rearrange("a j i t -> j (a i) t"),
                                         grid[:, half]).then_inc(stored[half], 16)
                    if nxt is None:
                        for half in range(2):
                            sp.wait_ge(stored[half], TILES * 16 + 1)

        step("first", 0, None)
        with nc.Fori(0, TILES - 1) as m:
            step("middle", m + 1, m)
        step("last", None, TILES - 1)
        nc.all_engine_barrier(sems_to_clear=range(FIRST_SEM - 2, FIRST_SEM))
        for sem in stored:
            nc.release_semaphore(sem)


def experts(nc, s, layer, hi, lo):
    PAIRS = N_KEYS // 2
    with ExitStack() as mem:
        def sb(name, shape, dt=F32):
            return mem.enter_context(nc.sbuf_tensor("ex_" + name, shape, dt))

        y = sb("y", [P, KB, T])
        u_raw, u_hi, u_lo = sb("u_raw", [P, 2, KB, P]), sb("u_hi", [P, 2, KB, P], F32R), sb("u_lo", [P, 2, KB, P], F32R)
        v_raw, v_hi, v_lo = sb("v_raw", [P, 2, D]), sb("v_hi", [P, 4, D], F32R), sb("v_lo", [P, 4, D], F32R)
        g = sb("g", [P, 2, 2 * TILES, 2, P // 2])
        act_e, wa = sb("act_e", [P, 2, T]), sb("wa", [P, 2, T])
        wa_hi, wa_lo = sb("wa_hi", [P, 4, T], F32R), sb("wa_lo", [P, 4, T], F32R)
        ps_a = mem.enter_context(nc.psum_tensor("ex_ps_a", [P, 2, 2, 512], F32))
        ps_y = mem.enter_context(nc.psum_tensor("ex_ps_y", [P, 2, 2, 512], F32))
        names = ["u_in0", "u_in1", "v_in0", "v_in1", "g_in0", "g_in1", "u_hi", "u_split", "v_hi", "v_split", "a_done",
                 "gelu", "wa", "wa_hi", "wa_split", "y_done", "y_added"]
        with stage(nc, *["ex_" + n for n in names]) as (block, *sems):
            e = dict(zip(names, sems))
            u_in, v_in, g_in = (e["u_in0"], e["u_in1"]), (e["v_in0"], e["v_in1"]), (e["g_in0"], e["g_in1"])

            @block.sync
            def _(sp):
                with sp.Fori(0, PAIRS // 2) as i:
                    for n in range(4):
                        r, k = n // 2, n % 2
                        row = layer * N_KEYS + i * 4 + n
                        sp.wait_ge(e["u_split"], i * 4 + n + 1)
                        sp.dma_start(u_raw[:, k], s.d["expert_u"][bass.ds(row, 1)]
                                     .rearrange("a p k n -> p (a k) n")).then_inc(u_in[k], 16)
                        sp.wait_ge(e["v_split"], i * 4 + n + 1)
                        sp.dma_start(v_raw[:, k], s.d["expert_v"][bass.ds(row, 1)]
                                     .rearrange("a p n -> p (a n)")).then_inc(v_in[k], 16)
                        if k == 0:
                            continue
                        sp.wait_ge(e["wa"], i * 4 + 2 * r + 1)
                        sp.dma_start(g[:, r].rearrange("p n a t -> p n (a t)"), 
                                     s.d["grid"][:, :, bass.ds(i * 4 + 2 * r, 2), :]
                                     .rearrange("n j a t -> j n (a t)")).then_inc(g_in[r], 16)

            def split_hi(act, i, slots):
                for k in range(2):
                    act.wait_ge(u_in[k], (i + 1) * 16)
                    act.wait_ge(e["a_done"], i * 2 + k + 1)
                    nc.scalar.activation(u_hi[:, k], u_raw[:, k], ACT.Copy).then_inc(e["u_hi"], 1)
                for k in range(2):
                    act.wait_ge(v_in[k], (i + 1) * 16)
                    act.wait_ge(e["y_done"], i * KB + KB)
                    nc.scalar.activation(v_hi[:, slots + k], v_raw[:, k], ACT.Copy).then_inc(e["v_hi"], 1)

            def weigh_hi(act, i, k, slot):
                act.wait_ge(e["a_done"], i * 2 + k + 3)
                act.wait_ge(e["wa"], i * 2 + k + 1)
                nc.scalar.activation(act_e[:, k].rearrange("p (q n) -> p q n", q=2), ps_a[:, k, :, 0:HALF],
                                     ACT.Gelu_apprx_tanh).then_inc(e["gelu"], 1)
                act.wait_ge(e["wa"], i * 2 + k + 3)
                act.wait_ge(e["y_done"], i * KB + KB)
                nc.scalar.activation(wa_hi[:, slot], wa[:, k], ACT.Copy).then_inc(e["wa_hi"], 1)

            @block.scalar
            def _(act):
                split_hi(act, 0, 0)
                with act.Fori(0, PAIRS // 2 - 1) as i:
                    for r in range(2):
                        for k in range(2):
                            weigh_hi(act, i * 2 + r, k, 2 * r + k)
                        split_hi(act, i * 2 + (r + 1), 2 * (1 - r))
                for k in range(2):
                    weigh_hi(act, PAIRS - 2, k, k)
                split_hi(act, PAIRS - 1, 2)
                for k in range(2):
                    weigh_hi(act, PAIRS - 1, k, 2 + k)

            @block.gpsimd
            def _(pool):
                pool.sem_inc(e["u_split"], 2)
                pool.sem_inc(e["v_split"], 2)
                with pool.Fori(0, PAIRS // 2) as i:
                    for r in range(2):
                        for k in range(2):
                            pool.wait_ge(e["u_hi"], i * 4 + (2 * r + k + 1))
                            nc.gpsimd.tensor_tensor(u_lo[:, k], u_raw[:, k], u_hi[:, k].bitcast(F32),
                                                    ALU.subtract).then_inc(e["u_split"], 1)
                        for k in range(2):
                            pool.wait_ge(e["v_hi"], i * 4 + (2 * r + k + 1))
                            nc.gpsimd.tensor_tensor(v_lo[:, 2 * r + k], v_raw[:, k], v_hi[:, 2 * r + k].bitcast(F32),
                                                    ALU.subtract).then_inc(e["v_split"], 1)

            def weigh(dve, i, k, slot):
                dve.wait_ge(e["gelu"], i * 2 + k + 1)
                dve.wait_ge(e["wa_split"], i * 2 + k + 1)
                nc.vector.tensor_tensor(wa[:, k].rearrange("p (n t) -> p n t", t=P // 2),
                                        act_e[:, k].rearrange("p (n t) -> p n t", t=P // 2),
                                        g[:, slot // 2, :, k, :], ALU.mult).then_inc(e["wa"], 1)

            def weigh_lo(dve, i, k, slot):
                dve.wait_ge(e["wa_hi"], i * 2 + k + 1)
                nc.vector.tensor_tensor(wa_lo[:, slot], wa[:, k], wa_hi[:, slot].bitcast(F32),
                                        ALU.subtract).then_inc(e["wa_split"], 1)

            def add_y(dve, i, blocks):
                for b in blocks:
                    dve.wait_ge(e["y_done"], i * KB + (2 * KB + b + 1))
                    yb = y[:, b].rearrange("p (q n) -> p q n", q=2)
                    nc.vector.tensor_tensor(yb, yb, ps_y[:, b % 2, :, 0:HALF], ALU.add).then_inc(e["y_added"], 1)

            @block.vector
            def _(dve):
                dve.sem_inc(e["wa"], 2)
                dve.sem_inc(e["wa_split"], 2)
                nc.vector.memset(y[:], 0.0).then_inc(e["y_added"], 1)

                def pair(i, slots, turn, before=None):
                    dve.wait_ge(g_in[slots // 2], turn * 16 + 16)
                    weigh(dve, i, 0, slots)
                    weigh_lo(dve, i, 0, slots)
                    weigh(dve, i, 1, slots + 1)
                    if before is not None:
                        add_y(dve, before, (0, 1))
                    weigh_lo(dve, i, 1, slots + 1)
                    if before is not None:
                        add_y(dve, before, range(2, KB))

                dve.wait_ge(e["y_added"], 1)
                dve.sem_inc(e["y_added"], 1)
                pair(0, 0, 0)
                with dve.Fori(0, PAIRS // 2 - 1) as i:
                    pair(i * 2 + 1, 2, i, i * 2)
                    pair(i * 2 + 2, 0, i + 1, i * 2 + 1)
                pair(PAIRS - 1, 2, PAIRS // 2 - 1, PAIRS - 2)
                add_y(dve, PAIRS - 1, range(KB))
                dve.wait_ge(e["y_added"], PAIRS * KB + 2)
                for b in range(KB):
                    for c, a, z in SEGMENTS:
                        nc.vector.scalar_tensor_tensor(s.x[:, b, a:z], y[:, b, a:z], s.mod[:, 5 * KB + b, c:c + 1],
                                                       s.x[:, b, a:z], ALU.mult, ALU.add)

            @block.tensor
            def _(pe):
                pe.sem_inc(e["a_done"], 2)
                pe.sem_inc(e["y_done"], 2 * KB)

                def first(i):
                    for k in range(2):
                        pe.wait_ge(e["u_split"], i * 2 + k + 3)
                        pe.wait_ge(e["wa"], i * 2 + k + 1)
                        for kb in range(KB):
                            last = matmul_split(nc, ps_a[:, k], u_hi[:, k, kb], u_lo[:, k, kb], hi[:, kb], lo[:, kb],
                                                kb == 0, kb == KB - 1)
                        last.then_inc(e["a_done"], 1)

                def second(i, slots):
                    pe.wait_ge(e["v_split"], i * 2 + 4)
                    pe.wait_ge(e["wa_split"], i * 2 + 4)
                    for b in range(KB):
                        pe.wait_ge(e["y_added"], i * KB + b + 1)
                        for k in range(2):
                            n = slots + k
                            c = slice(b * P, (b + 1) * P)
                            last = matmul_split(nc, ps_y[:, b % 2], v_hi[:, n, c], v_lo[:, n, c], wa_hi[:, n],
                                                wa_lo[:, n], k == 0, k == 1)
                        last.then_inc(e["y_done"], 1)

                first(0)
                with pe.Fori(0, PAIRS // 2 - 1) as i:
                    first(i * 2 + 1)
                    second(i * 2, 0)
                    first(i * 2 + 2)
                    second(i * 2 + 1, 2)
                first(PAIRS - 1)
                second(PAIRS - 2, 0)
                second(PAIRS - 1, 2)


def build(nc, d):
    with ExitStack() as mem:
        def sb(name, *shape):
            return mem.enter_context(nc.sbuf_tensor(name, [P, *shape], F32))

        s = Names()
        s.d = d
        s.x = sb("x", KB, T)
        s.ones, s.blk, s.ident = sb("ones", P), sb("blk", P), sb("ident", P)
        s.silu_parts = mem.enter_context(nc.sbuf_tensor("silu_parts", [P, KB, 4], F32R))
        s.mod, s.gain1, s.gain2 = sb("mod", 48, 2), sb("gain1", KB, 2), sb("gain2", KB, 2)
        s.pv = sb("pv", NPV)
        s.pvs = lambda n: s.pv[:, PV[n][0]:PV[n][1]]
        load_constants(nc, s)
        with nc.Fori(0, LAYERS) as layer:
            modulation(nc, s, layer)
            with ExitStack() as mixers:
                s.z = mixers.enter_context(nc.sbuf_tensor("z", [P, IN_BLOCKS, T], F32))
                with nc.sbuf_tensor("h1_hi", [P, KB, T], F32R) as hi, nc.sbuf_tensor("h1_lo", [P, KB, T], F32R) as lo:
                    rms_modulate(nc, s, "n1", s.gain1, 0, hi, lo)
                    input_projection(nc, s, layer, hi, lo)
                s.mix = mixers.enter_context(nc.sbuf_tensor("mix", [P, KB, T], F32))
                attention(nc, s, layer)
                rwkv(nc, s, layer)
                with nc.sbuf_tensor("m_hi", [P, KB, T], F32R) as hi, nc.sbuf_tensor("m_lo", [P, KB, T], F32R) as lo:
                    split_mix(nc, s, hi, lo)
                    output_projection(nc, s, layer, hi, lo)
            with nc.sbuf_tensor("h2_hi", [P, KB, T], F32R) as hi, nc.sbuf_tensor("h2_lo", [P, KB, T], F32R) as lo:
                rms_modulate(nc, s, "n2", s.gain2, 3 * KB, hi, lo)
                shape = [P, TILES, 2 * HEADS, TOPK]
                with nc.sbuf_tensor("best", shape, F32) as best, nc.sbuf_tensor("best_f", shape, BF16) as best_f:
                    query_scores(nc, s, layer, hi, lo, best, best_f)
                    retrieve(nc, s, best, best_f)
                experts(nc, s, layer, hi, lo)
        with stage(nc, "x_stored") as (block, stored):
            @block.sync
            def _(sp):
                sp.dma_start(d["x_out"], s.x[:]).then_inc(stored, 16)
                sp.wait_ge(stored, 16)



def rope_tables():
    quarter = HD // 4
    freqs = (10000.0 ** (-np.arange(quarter, dtype=np.float32) / np.float32(quarter))).astype(np.float32)
    tok = np.arange(LAT)
    table = np.zeros((HD, 2, LAT), np.float32)
    swap = np.zeros((HD, HD), np.float32)
    for f in range(HD):
        part, i = f // (2 * quarter), f % (2 * quarter)
        pos = (tok // 64 if part == 0 else tok % 64).astype(np.float32)
        ang = pos * freqs[i % quarter]
        table[f, 0], table[f, 1] = np.cos(ang), np.sin(ang)
        if i < quarter:
            swap[f + quarter, f] = -1.0
        else:
            swap[f - quarter, f] = 1.0
    return np.concatenate([table, table]), np.kron(np.eye(2, dtype=np.float32), swap)


def attention_masks():
    neg = np.float32(-1e30)
    out = np.full((TILES, P, 4, P), neg, np.float32)
    out[0, :, 0] = 0.0
    q, k = np.arange(P)[:, None], np.arange(P)[None, :]
    for j in range(LAT // P):
        for o in (-1, 0, 1):
            if 0 <= j + o < LAT // P:
                out[j + 1, :, o + 1] = np.where(np.abs(q - (k + o * P)) <= 128, np.float32(0), neg)
        out[j + 1, :, 3] = 0.0
    return out.reshape(TILES, P, 4 * P)


def rwkv_constants():
    a, b = np.arange(CHUNK)[:, None], np.arange(CHUNK)[None, :]
    masks = np.zeros((2, 10, CHUNK, CHUNK), np.float32)
    tri = np.zeros((2, P, 2, P), np.float32)
    for d in range(2):
        before = (a < b) if d == 0 else (a > b)
        upto = before | (a == b)

        def level(n):
            return ((a >> (n + 1)) == (b >> (n + 1))) & ((a >> n) != (b >> n)) & before

        masks[d, 0] = before
        masks[d, 1] = -1.0 * upto
        masks[d, 2] = upto
        masks[d, 3] = -1.0 * level(0).T
        masks[d, 4] = -1.0 * level(0)
        for n in range(1, LEVELS):
            masks[d, 4 + n] = level(n)
        for c in range(2):
            tri[d, 64 * c:64 * c + 64, 0, 64 * c:64 * c + 64] = upto
            tri[d, 64 * c:64 * c + 64, 1, 64 * c:64 * c + 64] = before
    masks = np.tile(masks.transpose(2, 0, 1, 3), (2, 1, 1, 1))
    keep = np.ones((2, TILES), np.float32)
    keep[0, 0] = keep[0, 1] = keep[1, 0] = keep[1, TILES - 1] = 0.0
    return (masks, tri.transpose(1, 0, 2, 3).reshape(P, 2, 2 * P), np.tile(np.eye(CHUNK, dtype=np.float32), (2, 1)),
            np.tile(keep.reshape(1, -1), (P, 1)))


def layout(x):
    def feat(a):
        return a.reshape(LAYERS, -1, P).transpose(0, 2, 1)

    def rep(a):
        return np.broadcast_to(a[:, None, :], (LAYERS, P, a.shape[1]))

    def blocks(w, width=P):
        n = w.shape[2] // width
        return w.reshape(LAYERS, KB, P, n, width).transpose(0, 3, 2, 1, 4)

    pairs = np.concatenate([np.r_[b * HD:(b + 1) * HD, (b + 4) * HD:(b + 5) * HD] for b in range(4)])
    w_in = x["w_in"][:, :, np.r_[pairs, 512:x["w_in"].shape[2]]]
    w_out = x["w_out"][:, np.r_[pairs, 512:D], :]
    o = {}
    tok = np.concatenate([x["x_prompt"][0], x["x_sample"][0]])
    o["x_in"] = tok.T.reshape(KB, P, T).transpose(1, 0, 2)
    o["cond"] = np.stack([x["c_ctx"], x["c"][0]]).reshape(2, KB, P).transpose(2, 1, 0)
    o["w_blocks"] = np.concatenate([blocks(w_in), blocks(w_out), blocks(x["w_query"])], 1).reshape(-1, P, KB, P)
    o["w_mod"] = blocks(x["w_mod"], 4 * P).reshape(-1, P, KB, 4 * P)
    conv = x["conv_rkv"].reshape(LAYERS, 36, P).transpose(0, 2, 1)
    o["pv"] = np.concatenate([
        feat(x["norm1"]), feat(x["norm2"]), np.tile(x["q_norm"], (1, 2))[:, :, None],
        np.tile(x["k_norm"], (1, 2))[:, :, None], conv, feat(x["a0"].reshape(LAYERS, -1)), feat(x["k_k"]),
        feat(x["k_a"]), feat(x["r_k"].reshape(LAYERS, -1)), feat(x["ln_x_g"]), feat(x["ln_x_b"]), feat(x["b_mod"]),
        rep(x["sink"])], 2)
    o["w0"] = rep(x["w0"].reshape(LAYERS, -1))
    o["w2"], o["a2"] = x["w2"].reshape(LAYERS, P, D_R), x["a2"].reshape(LAYERS, P, D_R)
    o["g2"] = x["g2"]
    o["cache_k"] = x["cache_k"][0].reshape(LAYERS, P, P).transpose(0, 2, 1)
    o["cache_v"] = x["cache_v"][0].reshape(LAYERS, P, P)
    st = x["state_rwkv"][0].reshape(LAYERS, 2, RB, 2, HD, HD).transpose(0, 1, 3, 5, 2, 4).reshape(LAYERS, 2, P, 256)
    init = np.zeros((LAYERS, 2, TILES, P, 256), np.float32)
    init[:, 0, 1], init[:, 1, 0] = st[:, 0], st[:, 1]
    o["state_in"] = init.reshape(-1, P, 256)
    o["sub_keys"] = x["sub_keys"].transpose(0, 3, 1, 2)
    o["expert_u"] = x["expert_u"].reshape(LAYERS, N_KEYS, P, KB, P).transpose(0, 1, 4, 3, 2).reshape(-1, P, KB, P)
    o["expert_v"] = x["expert_v"].reshape(-1, P, D)
    o["rope"], o["swap"] = rope_tables()
    o["masks"] = attention_masks()
    o["r_masks"], o["tri"], o["ident2"], o["keep"] = rwkv_constants()
    o["ones"], o["ident"] = np.ones((P, P), np.float32), np.eye(P, dtype=np.float32)
    o["blk"] = np.kron(np.eye(2, dtype=np.float32), np.ones((HD, HD), np.float32))
    o["iota"] = np.tile(np.arange(P, dtype=np.float32), (P, 1))
    return {k: np.ascontiguousarray(v, dtype=v.dtype) for k, v in o.items()}


OUTS = {"x_out": (P, KB, T), "kv_out": (LAYERS, P, 2, CTX), "state_out": (LAYERS * 2 * TILES, P, 256)}


def kernel(**inputs):
    import concourse.bacc as bacc
    from concourse.bass_utils import run_bass_kernel_spmd

    arrays = layout({k: np.asarray(v) for k, v in inputs.items()})
    nc = bacc.Bacc("TRN2", target_bir_lowering=False, num_devices=1)
    dram = {name: nc.dram_tensor("in_" + name, a.shape, mybir.dt.from_np(a.dtype), kind="ExternalInput").ap()
            for name, a in arrays.items()}
    for name, shape in OUTS.items():
        dram[name] = nc.dram_tensor("out_" + name, shape, F32, kind="ExternalOutput").ap()
    dram["grid"] = nc.dram_tensor("grid_scratch", (2 * TILES, P, N_KEYS, P // 2), F32, kind="Internal").ap()
    build(nc, dram)
    r = run_bass_kernel_spmd(nc, [{"in_" + k: a for k, a in arrays.items()}], core_ids=[0]).results[0]

    tok = r["out_x_out"].transpose(2, 1, 0).reshape(T, D)
    kv = r["out_kv_out"].transpose(2, 0, 3, 1)
    kv = kv.reshape(2, 1, LAYERS, CTX, 2, HD)
    st = r["out_state_out"].reshape(LAYERS, 2, TILES, 2, HD, RB, HD)
    st = np.stack([st[:, 0, 0], st[:, 1, TILES - 1]], 1).transpose(0, 1, 4, 2, 5, 3)
    st = st.reshape(1, LAYERS, 2, HEADS, HD, HD)
    return (tok[None, :CTX], tok[None, CTX:], kv[0], kv[1], st)
```
